# Optimizing a Trainium2 kernel written in Bass

```python
import jax, jax.numpy as jnp
from jax import lax
import numpy as np

D_MODEL = 1024
BATCH = 1
SEQ = 256
DEPTH = 2
DEC_BATCH = 1
DEC_SEQ = 32
PAST_LEN = 256

CHUNK = 64
BLOCK = 16
GLA_HEADS = 4
GLA_DK = 48
GLA_DV = 96
GLA_GATE_RANK = 16
GLA_TAU = 16.0
HG_HEADS = 4
HG_DK = 64
HG_DV = 96
RG_WIDTH = 256
RG_BLOCKS = 4
RG_BLOCK_DIM = RG_WIDTH // RG_BLOCKS
RG_CONV = 4
RG_C = 8.0
MIX_WIDTH = GLA_HEADS * GLA_DV + HG_HEADS * HG_DV + RG_WIDTH
MEM_LEN = 256
XA_HEADS = 4
XA_DH = D_MODEL // XA_HEADS
D_FF = 2816
N_EXPERTS = 8
TOP_K = 2
N_DENSE = (DEPTH + 1) // 2
N_MOE = DEPTH // 2
EPS = 1e-6
IN_SIZES = (GLA_HEADS * GLA_DK, GLA_HEADS * GLA_DK, GLA_HEADS * GLA_DV, GLA_HEADS * GLA_DV, GLA_GATE_RANK,
            HG_HEADS * HG_DK, HG_HEADS * HG_DK, HG_HEADS * HG_DV, HG_HEADS * HG_DV,
            RG_WIDTH, RG_WIDTH)
IN_WIDTH = sum(IN_SIZES)

kernel_name = 'hymba_gla_hgrn2_rglru_stream_step'

def rms_norm(x, g):
    xf = x.astype(jnp.float32)
    y = xf * lax.rsqrt(jnp.mean(xf * xf, axis=-1, keepdims=True) + EPS)
    return (y * g.astype(jnp.float32)).astype(x.dtype)

def head_rms(o, g):
    B, T, H, V = o.shape
    of = o.astype(jnp.float32)
    of = of * lax.rsqrt(jnp.mean(of * of, axis=-1, keepdims=True) + EPS)
    return (of.reshape(B, T, H * V) * g.astype(jnp.float32)).astype(o.dtype)

def gated_recurrence(q, k, v, log_g, s0):
    B, T, H, K = q.shape
    V = v.shape[-1]
    f32 = jnp.float32
    pad = (-T) % BLOCK
    padt = lambda a: jnp.pad(a.astype(f32), ((0, 0), (0, pad), (0, 0), (0, 0)))
    n = (T + pad) // BLOCK
    blk = lambda a: padt(a).reshape(B, n, BLOCK, H, a.shape[-1])
    qb, kb, vb, lg = blk(q), blk(k), blk(v), blk(log_g)
    b = jnp.cumsum(lg, axis=2)
    causal = jnp.tril(jnp.ones((BLOCK, BLOCK), bool))[None, None, :, :, None, None]
    diff = b[:, :, :, None] - b[:, :, None]
    decay = jnp.where(causal, jnp.exp(jnp.where(causal, diff, 0.0)), 0.0)
    scores = jnp.einsum('bnthk,bnshk,bntshk->bntsh', qb, kb, decay)
    o_intra = jnp.einsum('bntsh,bnshv->bnthv', scores, vb)
    b_last = b[:, :, -1]
    k_dec = kb * jnp.exp(b_last[:, :, None] - b)
    q_dec = qb * jnp.exp(b)

    def step(S, inp):
        bl, kd, vv = inp
        S_new = jnp.exp(bl)[..., None] * S + jnp.einsum('blhk,blhv->bhkv', kd, vv)
        return S_new, S

    xs = (jnp.moveaxis(b_last, 1, 0), jnp.moveaxis(k_dec, 1, 0), jnp.moveaxis(vb, 1, 0))
    S_T, S_prev = lax.scan(step, s0.astype(f32), xs)
    o_inter = jnp.einsum('bnlhk,nbhkv->bnlhv', q_dec, S_prev)
    o = (o_intra + o_inter).reshape(B, n * BLOCK, H, V)[:, :T]
    return o.astype(v.dtype), S_T.astype(s0.dtype)

def gla_mixer(q, k, v, r, a_low, wa2, ba, onorm, s0):
    B, T, _ = q.shape
    q = q.reshape(B, T, GLA_HEADS, GLA_DK) * (GLA_DK ** -0.5)
    k = k.reshape(B, T, GLA_HEADS, GLA_DK)
    v = v.reshape(B, T, GLA_HEADS, GLA_DV)
    log_a = jax.nn.log_sigmoid((a_low @ wa2 + ba).astype(jnp.float32)) / GLA_TAU
    o, s = gated_recurrence(q, k, v, log_a.reshape(B, T, GLA_HEADS, GLA_DK), s0)
    return head_rms(o, onorm) * jax.nn.silu(r), s

def hgrn2_mixer(q, f_pre, i, g, lb, onorm, s0):
    B, T, _ = q.shape
    z = f_pre.astype(jnp.float32)
    sig = jax.nn.sigmoid(z)
    f = lb + (1.0 - lb) * sig
    log_f = jnp.log(f)
    k = (1.0 - lb) * jax.nn.sigmoid(-z)
    q = jax.nn.silu(q).reshape(B, T, HG_HEADS, HG_DK)
    o, s = gated_recurrence(q, k.reshape(B, T, HG_HEADS, HG_DK), i.reshape(B, T, HG_HEADS, HG_DV),
                            log_f.reshape(B, T, HG_HEADS, HG_DK), s0)
    return head_rms(o, onorm) * jax.nn.silu(g), s

def rglru_mixer(xb, gb, conv_w, conv_b, wr, br, wi, bi, lam, h0, conv0):
    B, T, W = xb.shape
    xc = jnp.concatenate([conv0.astype(xb.dtype), xb], axis=1)
    new_conv = xc[:, -(RG_CONV - 1):]
    u = conv_b
    for j in range(RG_CONV):
        u = u + xc[:, j:j + T] * conv_w[j]
    ub = u.reshape(B, T, RG_BLOCKS, RG_BLOCK_DIM)
    r = jax.nn.sigmoid(jnp.einsum('btnc,ncd->btnd', ub, wr).reshape(B, T, W) + br).astype(jnp.float32)
    ig = jax.nn.sigmoid(jnp.einsum('btnc,ncd->btnd', ub, wi).reshape(B, T, W) + bi).astype(jnp.float32)
    log_a = -RG_C * r * jax.nn.softplus(-lam.astype(jnp.float32))
    a = jnp.exp(log_a)
    beta = jnp.sqrt(jnp.maximum(-jnp.expm1(2.0 * log_a), 1e-12))
    bterm = beta * (ig * u.astype(jnp.float32))
    bterm = bterm.at[:, 0].add(a[:, 0] * h0.astype(jnp.float32))

    def comb(e1, e2):
        a1, b1 = e1
        a2, b2 = e2
        return a1 * a2, a2 * b1 + b2

    _, h = lax.associative_scan(comb, (a, bterm), axis=1)
    y = h.astype(xb.dtype) * jax.nn.gelu(gb)
    return y, h[:, -1].astype(h0.dtype), new_conv.astype(conv0.dtype)

def mem_kv(mem, g, wk, wv):
    B, M, _ = mem.shape
    m = rms_norm(mem, g)
    return (m @ wk).reshape(B, M, XA_HEADS, XA_DH), (m @ wv).reshape(B, M, XA_HEADS, XA_DH)

def mem_attend(h, k, v, wq, wo):
    B, T, _ = h.shape
    q = (h @ wq).reshape(B, T, XA_HEADS, XA_DH)
    s = jnp.einsum('bthd,bmhd->bhtm', q, k).astype(jnp.float32) * (XA_DH ** -0.5)
    p = jax.nn.softmax(s, axis=-1).astype(v.dtype)
    o = jnp.einsum('bhtm,bmhd->bthd', p, v).reshape(B, T, D_MODEL)
    return o @ wo

def swiglu(h, w1, w3, w2):
    return (jax.nn.silu(h @ w1) * (h @ w3)) @ w2

def moe(h, router, w1, w3, w2):
    logits = (h @ router).astype(jnp.float32)
    top_v, top_i = lax.top_k(logits, TOP_K)
    gates = jax.nn.softmax(top_v, axis=-1)
    dense_gate = jnp.sum(jax.nn.one_hot(top_i, N_EXPERTS, dtype=jnp.float32) * gates[..., None], axis=-2)
    out = jnp.zeros_like(h)
    for e in range(N_EXPERTS):
        out = out + dense_gate[..., e:e + 1].astype(h.dtype) * swiglu(h, w1[e], w3[e], w2[e])
    return out

def trunk(x, mem_k, mem_v, s_gla, s_hg, s_rg, s_conv, W):
    p = jax.nn.softmax(W['hg_lb'].astype(jnp.float32), axis=0)
    lb_all = jnp.cumsum(p, axis=0) - p[:1]
    points = [sum(IN_SIZES[:j + 1]) for j in range(len(IN_SIZES) - 1)]
    n_gla, n_hg, n_rg, n_cv = [], [], [], []
    for l in range(DEPTH):
        h = rms_norm(x, W['norm_mix'][l])
        gq, gk, gv, gr, ga, hq, hf, hi, hgate, rx, rgate = jnp.split(h @ W['w_in'][l], points, axis=-1)
        o_gla, sg = gla_mixer(gq, gk, gv, gr, ga, W['gla_wa2'][l], W['gla_ba'][l], W['gla_onorm'][l], s_gla[l])
        o_hg, sh = hgrn2_mixer(hq, hf, hi, hgate, lb_all[l], W['hg_onorm'][l], s_hg[l])
        o_rg, sr, sc = rglru_mixer(rx, rgate, W['rg_conv_w'][l], W['rg_conv_b'][l], W['rg_wr'][l], W['rg_br'][l],
                                   W['rg_wi'][l], W['rg_bi'][l], W['rg_lambda'][l], s_rg[l], s_conv[l])
        x = x + jnp.concatenate([o_gla, o_hg, o_rg], axis=-1) @ W['w_out'][l]
        h = rms_norm(x, W['norm_xattn'][l])
        x = x + mem_attend(h, mem_k[l], mem_v[l], W['xa_wq'][l], W['xa_wo'][l])
        h = rms_norm(x, W['norm_ffn'][l])
        if l % 2 == 0:
            j = l // 2
            x = x + swiglu(h, W['ffd_w1'][j], W['ffd_w3'][j], W['ffd_w2'][j])
        else:
            j = l // 2
            x = x + moe(h, W['moe_router'][j], W['moe_w1'][j], W['moe_w3'][j], W['moe_w2'][j])
        n_gla.append(sg)
        n_hg.append(sh)
        n_rg.append(sr)
        n_cv.append(sc)
    y = rms_norm(x, W['norm_final'])
    return y, jnp.stack(n_gla), jnp.stack(n_hg), jnp.stack(n_rg), jnp.stack(n_cv)

def setup_inputs(seed: int = 0) -> dict:
    key = jax.random.key(seed)
    keys = jax.random.split(key, 40)
    f32 = jnp.float32
    L = DEPTH

    def nrm(i, shape, scale):
        return jax.random.normal(keys[i], shape, f32) * scale

    def gain(i, shape):
        return 1.0 + nrm(i, shape, 0.02)

    u = jax.random.uniform(keys[26], (L, RG_WIDTH), f32, 0.9, 0.999)
    a8 = u ** (1.0 / RG_C)
    rg_lambda = jnp.log(a8) - jnp.log1p(-a8)
    return {
        'x_prompt': nrm(0, (BATCH, SEQ, D_MODEL), 1.0),
        'x_sample': nrm(1, (DEC_BATCH, DEC_SEQ, D_MODEL), 1.0),
        'state_gla': nrm(2, (L, DEC_BATCH, GLA_HEADS, GLA_DK, GLA_DV), 1.0),
        'state_hgrn': nrm(3, (L, DEC_BATCH, HG_HEADS, HG_DK, HG_DV), 0.5),
        'state_rglru': nrm(4, (L, DEC_BATCH, RG_WIDTH), 0.5),
        'state_conv': nrm(5, (L, DEC_BATCH, RG_CONV - 1, RG_WIDTH), 1.0),
        'cache_mem_k': nrm(6, (L, DEC_BATCH, MEM_LEN, XA_HEADS, XA_DH), 1.0),
        'cache_mem_v': nrm(7, (L, DEC_BATCH, MEM_LEN, XA_HEADS, XA_DH), 1.0),
        'mem_prompt': nrm(8, (BATCH, MEM_LEN, D_MODEL), 1.0),
        'norm_mix': gain(9, (L, D_MODEL)),
        'norm_xattn': gain(10, (L, D_MODEL)),
        'norm_ffn': gain(11, (L, D_MODEL)),
        'norm_mem': gain(12, (L, D_MODEL)),
        'norm_final': gain(13, (D_MODEL,)),
        'w_in': nrm(14, (L, D_MODEL, IN_WIDTH), D_MODEL ** -0.5),
        'gla_wa2': nrm(15, (L, GLA_GATE_RANK, GLA_HEADS * GLA_DK), GLA_GATE_RANK ** -0.5),
        'gla_ba': nrm(16, (L, GLA_HEADS * GLA_DK), 0.1),
        'gla_onorm': gain(17, (L, GLA_HEADS * GLA_DV)),
        'hg_lb': nrm(18, (L, HG_HEADS * HG_DK), 0.5),
        'hg_onorm': gain(19, (L, HG_HEADS * HG_DV)),
        'rg_conv_w': nrm(20, (L, RG_CONV, RG_WIDTH), RG_CONV ** -0.5),
        'rg_conv_b': nrm(21, (L, RG_WIDTH), 0.02),
        'rg_wr': nrm(22, (L, RG_BLOCKS, RG_BLOCK_DIM, RG_BLOCK_DIM), RG_BLOCK_DIM ** -0.5),
        'rg_br': nrm(23, (L, RG_WIDTH), 0.1),
        'rg_wi': nrm(24, (L, RG_BLOCKS, RG_BLOCK_DIM, RG_BLOCK_DIM), RG_BLOCK_DIM ** -0.5),
        'rg_bi': nrm(25, (L, RG_WIDTH), 0.1),
        'rg_lambda': rg_lambda,
        'w_out': nrm(27, (L, MIX_WIDTH, D_MODEL), MIX_WIDTH ** -0.5),
        'xa_wq': nrm(28, (L, D_MODEL, D_MODEL), D_MODEL ** -0.5),
        'xa_wk': nrm(29, (L, D_MODEL, D_MODEL), D_MODEL ** -0.5),
        'xa_wv': nrm(30, (L, D_MODEL, D_MODEL), D_MODEL ** -0.5),
        'xa_wo': nrm(31, (L, D_MODEL, D_MODEL), D_MODEL ** -0.5),
        'ffd_w1': nrm(32, (N_DENSE, D_MODEL, D_FF), D_MODEL ** -0.5),
        'ffd_w3': nrm(33, (N_DENSE, D_MODEL, D_FF), D_MODEL ** -0.5),
        'ffd_w2': nrm(34, (N_DENSE, D_FF, D_MODEL), D_FF ** -0.5),
        'moe_router': nrm(35, (N_MOE, D_MODEL, N_EXPERTS), D_MODEL ** -0.5),
        'moe_w1': nrm(36, (N_MOE, N_EXPERTS, D_MODEL, D_FF), D_MODEL ** -0.5),
        'moe_w3': nrm(37, (N_MOE, N_EXPERTS, D_MODEL, D_FF), D_MODEL ** -0.5),
        'moe_w2': nrm(38, (N_MOE, N_EXPERTS, D_FF, D_MODEL), D_FF ** -0.5),
    }

def reference(x_prompt, x_sample, state_gla, state_hgrn, state_rglru, state_conv, cache_mem_k, cache_mem_v,
              mem_prompt, norm_mix, norm_xattn, norm_ffn, norm_mem, norm_final, w_in, gla_wa2, gla_ba,
              gla_onorm, hg_lb, hg_onorm, rg_conv_w, rg_conv_b, rg_wr, rg_br, rg_wi, rg_bi, rg_lambda, w_out,
              xa_wq, xa_wk, xa_wv, xa_wo, ffd_w1, ffd_w3, ffd_w2, moe_router, moe_w1, moe_w3, moe_w2):
    W = dict(norm_mix=norm_mix, norm_xattn=norm_xattn, norm_ffn=norm_ffn, norm_final=norm_final,
             w_in=w_in, gla_wa2=gla_wa2, gla_ba=gla_ba, gla_onorm=gla_onorm, hg_lb=hg_lb, hg_onorm=hg_onorm,
             rg_conv_w=rg_conv_w, rg_conv_b=rg_conv_b, rg_wr=rg_wr, rg_br=rg_br, rg_wi=rg_wi, rg_bi=rg_bi,
             rg_lambda=rg_lambda, w_out=w_out, xa_wq=xa_wq, xa_wo=xa_wo,
             ffd_w1=ffd_w1, ffd_w3=ffd_w3, ffd_w2=ffd_w2,
             moe_router=moe_router, moe_w1=moe_w1, moe_w3=moe_w3, moe_w2=moe_w2)
    mks, mvs = [], []
    for l in range(DEPTH):
        mk, mv = mem_kv(mem_prompt, norm_mem[l], xa_wk[l], xa_wv[l])
        mks.append(mk)
        mvs.append(mv)
    mem_k_p = jnp.stack(mks)
    mem_v_p = jnp.stack(mvs)
    dt = x_prompt.dtype
    z_gla = jnp.zeros((DEPTH, BATCH, GLA_HEADS, GLA_DK, GLA_DV), dt)
    z_hg = jnp.zeros((DEPTH, BATCH, HG_HEADS, HG_DK, HG_DV), dt)
    z_rg = jnp.zeros((DEPTH, BATCH, RG_WIDTH), dt)
    z_cv = jnp.zeros((DEPTH, BATCH, RG_CONV - 1, RG_WIDTH), dt)
    y_prompt, gla_p, hgrn_p, rglru_p, conv_p = trunk(x_prompt, mem_k_p, mem_v_p, z_gla, z_hg, z_rg, z_cv, W)
    y_sample, gla_s, hgrn_s, rglru_s, conv_s = trunk(x_sample, cache_mem_k, cache_mem_v, state_gla, state_hgrn,
                                                     state_rglru, state_conv, W)
    return (y_prompt, y_sample, gla_p, hgrn_p, rglru_p, conv_p, mem_k_p, mem_v_p, gla_s, hgrn_s, rglru_s, conv_s)


_drawn_inputs = setup_inputs


def setup_inputs(seed=0):
    import zlib

    import numpy as np

    out = dict(_drawn_inputs(seed))
    spreads = {}
    factors = {'norm_mem': 2.907, 'norm_final': 2.746}
    for name, (base, spread) in spreads.items():
        noise = np.random.default_rng([zlib.crc32(name.encode()), seed]).standard_normal(out[name].shape)
        drawn = base * np.exp(spread * noise) if base else spread * noise
        out[name] = __import__('jax').numpy.asarray(drawn.astype(out[name].dtype))
    for name, factor in factors.items():
        out[name] = (out[name] * factor).astype(out[name].dtype)
    return out
```

```python
from contextlib import ExitStack

import numpy as np

import concourse.bass as bass
from concourse import mybir

F32 = mybir.dt.float32
F32R = mybir.dt.float32r
I32 = mybir.dt.int32
U32 = mybir.dt.uint32
ALU = mybir.AluOpType
ACT = mybir.ActivationFunctionType
AX = mybir.AxisListType

P = 128
D = 1024
KD = D // P
TP, TS = 256, 32
T = TP + TS
TILES = [(0, 128), (128, 128), (256, 32)]
LAYERS = 2
DK_G, DK_H, DV = 48, 64, 96
HEADS = 8
PAIRS = 4
RANK = 16
RG = 256
CONV = 4
MEM = 256
DFF = 2816
FT = DFF // P
STEPS = FT // 2
NE = 8
EPS = 1e-6
CH = 32
NCH = T // CH
LEVELS = [16, 8, 4, 2, 1]
C = 96
MAXR = 3

GQ, GK, GV, GR, GA, HQ, HF, HI, HGT, RX, RGT, INW = (
    0, 192, 384, 768, 1152, 1168, 1424, 1680, 2064, 2448, 2704, 2960)

SLOT = 2048
RING = 11
DSLOTS = 3
UNITS_E = 3 * STEPS
SPLITS = 3


def dense_units():
    units = []
    for l in range(LAYERS):
        for key, a, b in (("in", RX, RX + 256), ("in", RGT, RGT + 256), ("in", HF, HF + 256),
                          ("in", GR + 192, GA + RANK), ("in", HQ, HQ + 256),
                          ("in", GV, GV + 192), ("in", GV + 192, GV + 384),
                          ("in", HI, HI + 192), ("in", HI + 192, HI + 384),
                          ("in", GR, GR + 192), ("in", HGT, HGT + 192), ("in", HGT + 192, HGT + 384)):
            units.append((key, l, a, b))
        for key in ("wk", "wv"):
            for j in range(4):
                units.append((key, l, 256 * j, 256 * j + 256))
        for d in range(KD):
            units.append(("out", l, P * d, P * d + P))
        for key in ("wq", "wo"):
            for j in range(4):
                units.append((key, l, 256 * j, 256 * j + 256))
        if l == 0:
            for s in range(STEPS):
                units.append(("w1", l, 256 * s, 256 * s + 256))
                units.append(("w3", l, 256 * s, 256 * s + 256))
            for d in range(KD):
                for half in range(2):
                    units.append(("w2", l, d, half))
    return units


def chunk_plan():
    plan = [("par", "V")] * 2 + [("x", "V")] * 6 + [("mem", "A")] * 4
    for l in range(LAYERS):
        plan += [("rx", "A")] * 2 + [("rgt", "A")] * 2 + [("q", "A")] * 2 + [("k", "A")] * 2
        plan += [("hf", "A")] * 2 + [("ga", "A")] + [("gate", "A")] * 2 + [("hq", "A")] * 2
        plan += [("v", "A")] * 12 + [("gate", "A")] * 6
        plan += [("kv", "A")] * 5
        plan += [("kdt", "A")] * 3 + [("kv", "A")] * 11
        plan += [("oss", "A")] * 8
        plan += [("out", "V")] * 8
        plan += [("wq", "A")] * 8 + [("kt", "V")] * 8 + [("pt", "A")] * 6 + [("ox", "A")] * 8 + [("wo", "V")] * 8
        if l == 0:
            plan += [("h1", "A"), ("h3", "V")] * FT + [("dn", "V")] * 8
    plan += [("htok", "A")] * 6 + [("lg", "V"), ("rank", "V")]
    plan += [("y", "V")] * 6 + [("small", "V")]
    return plan


PLAN = chunk_plan()
CHUNK_NO = {}
for _i, (_tag, _e) in enumerate(PLAN):
    CHUNK_NO[_tag, sum(1 for t, _ in PLAN[:_i] if t == _tag)] = _i


def emptied(tag, n):
    i = CHUNK_NO[tag, n]
    return sum(1 for _, e in PLAN[:i + 1] if e == PLAN[i][1])


def layer_program(nc, x_prompt, x_sample, state_gla, state_hgrn, state_rglru, state_conv, cache_mem_k, cache_mem_v,
                  mem_prompt, norm_mix, norm_xattn, norm_ffn, norm_mem, norm_final, w_in, gla_wa2, gla_ba,
                  gla_onorm, hg_lb, hg_onorm, rg_conv_w, rg_conv_b, rg_wr, rg_br, rg_wi, rg_bi, rg_lambda, w_out,
                  xa_wq, xa_wk, xa_wv, xa_wo, ffd_w1, ffd_w3, ffd_w2, moe_router, moe_w1, moe_w3, moe_w2,
                  y_prompt, y_sample, gla_p, hgrn_p, rglru_p, conv_p, mem_k_p, mem_v_p, gla_s, hgrn_s, rglru_s,
                  conv_s):
    units = dense_units()
    at = {}
    with ExitStack() as ctx:
        def sb(name, shape, dt=F32):
            at[name] = (nc.sbuf_base + 31) // 32 * 32
            return ctx.enter_context(nc.sbuf_tensor(name, shape, dt))

        def over(name, shape, offset):
            return nc.alloc_sbuf_tensor_at(name, shape, F32R, offset=offset)

        def sem(name):
            return ctx.enter_context(nc.semaphore(name))

        def view(base, off, *dims):
            n = int(np.prod(dims))
            flat = base[:, off:off + n]
            if len(dims) == 1:
                return flat
            names = " ".join("abcd"[i] for i in range(len(dims)))
            return flat.rearrange(f"p ({names}) -> p {names}", **{"abcd"[i]: dims[i] for i in range(1, len(dims))})

        ring = sb("ring", [P, RING * SLOT])
        xT = sb("xT", [P, KD, T])
        hT = sb("hT", [P, KD, T])
        memT = sb("memT", [P, KD, MEM])
        wqk = sb("wqk", [P, 2, KD, 256])
        kp = sb("kp", [P, 2, D])
        vp = sb("vp", [P, 2, D])
        low = sb("low", [P, 9792])
        s_init = sb("s_init", [P, PAIRS, DV])
        s_fin = sb("s_fin", [P, 2, PAIRS, DV])
        ident = sb("ident", [P, P])
        ones = sb("ones", [P, P])
        tri = sb("tri", [P, P])
        iota_c = sb("iota_c", [P, C])
        iota_e = sb("iota_e", [P, 3, NE])
        restart = sb("restart", [P, T])
        masks = sb("masks", [P, 6, CH], U32)
        par = sb("par", [P, 124])
        par2 = sb("par2", [P, 20])
        wa2 = sb("wa2", [RANK, LAYERS, 256])
        wri = sb("wri", [P, 2, 2, P])
        router = sb("router", [P, KD, NE])
        rstd = sb("rstd", [P, T])
        small = sb("small", [P, 32])
        drv = sb("drv", [P, 64])
        att = sb("att", [P, 2, 16])
        epsc = sb("epsc", [P, 1])
        stage3 = sb("stage3", [32, P])
        nround = sb("nround", [1, 1], I32)
        ps = ctx.enter_context(nc.psum_tensor("ps", [P, 8, 512], F32))

        UP = DSLOTS * SLOT
        q_t = view(ring, UP, PAIRS, T)
        k_t = view(ring, UP + 1152, PAIRS, T)
        b_t = view(ring, UP + 2304, PAIRS, T)
        e_t = view(ring, UP + 3456, PAIRS, T)
        kl_t = view(ring, UP + 4608, PAIRS, T)
        ql_t = view(ring, UP + 5760, PAIRS, T)
        osq = view(ring, UP + 3456, HEADS, T)
        a_full = view(ring, UP + 6912, 3, 4, 2, P)
        s_all = view(ring, UP + 9984, 8, PAIRS, DV)
        memg = view(ring, UP + 13056, KD, MEM)
        xc = view(ring, UP + 15104, 2, CONV - 1 + TP + CONV - 1 + TS)
        u_t = view(ring, UP + 15104 + 588, 2, T)
        ktp = view(ring, UP, KD, MEM)
        kts = view(ring, UP + 2048, KD, MEM)
        qx = view(ring, UP + 4096, KD, T)
        ks = view(ring, UP + 6912, 2, D)
        vs = view(ring, UP + 8960, 2, D)
        pt = view(ring, UP + 11008, 8, T)
        prob = view(ring, UP + 13312, 2, 4, MEM)
        xtok = view(ring, UP, 3, D)
        mtok = view(ring, UP + 3072, 2, D)
        msq = view(ring, UP + 5120, D)
        stage = view(ring, UP + 6144, P)
        stage2 = view(ring, UP + 6272, P)
        act_t = view(ring, UP, FT, T)
        v_tok = view(low, 0, 3, HEADS * DV)
        o_t = view(low, 2304, HEADS, T)
        a_comp = view(low, 2304, 2, 3, 4, CH)
        kd_tok = view(low, 2304 + 768, 3, 512)
        gate = view(low, 4608, HEADS, T)
        la = view(low, 6912, 2, T)
        it_ = view(low, 7488, 2, T)
        tn = view(low, 8064, 2, T)
        gb = view(low, 8640, 2, T)
        gaT = view(low, 9216, T)
        sil0 = view(low, 0, 2, T)
        htok = view(low, 0, 3, D)
        a_tok = view(low, 4608, 2, 2 * P)
        sil = view(low, 5120, 2, 2 * P)
        y_sb = view(low, 5952, D)
        sel = view(low, 6976, 3, C)
        selT = view(low, 7264, T)
        lgt = view(low, 7936, 3, NE)
        oh1 = view(low, 7960, 3, NE)
        oh2 = view(low, 7984, 3, NE)
        gd = view(low, 8008, 3, NE)
        msel = view(low, 8032, 3, NE)
        tmp8 = view(low, 8056, 3, NE)
        cols = view(low, 8080, 40)
        gcol = view(low, 8120, 3)
        gs = view(low, 8124, 1)
        posr = view(low, 8128, 3, (MAXR + 1) * NE)
        ytok = view(low, 0, 3, D)
        hg_hi = over("hg_hi", [P, KD, C], at["low"] + 4 * 3072)
        hg_lo = over("hg_lo", [P, KD, C], at["low"] + 4 * 3840)
        a_hi = over("a_hi", [P, 2, 2, C], at["low"] + 4 * 8256)
        a_lo = over("a_lo", [P, 2, 2, C], at["low"] + 4 * 8640)
        w_hi = over("w_hi", [P, SPLITS * SLOT], at["hT"])
        w_lo = over("w_lo", [P, SPLITS * SLOT], at["hT"] + 4 * SPLITS * SLOT)

        c_mix, c_xa, c_ff, c_mem, c_fin = 0, 16, 32, 48, 64
        c_lb, c_cb, c_br, c_bi, c_lam, c_cw, c_h0, c_c0 = 72, 76, 80, 84, 88, 92, 108, 112
        v_kA, v_kB, v_fb, v_sp, v_br, v_bi, v_ms = 0, 4, 8, 12, 16, 20, 24

        unit_in = [sem(f"unit_in{i}") for i in range(DSLOTS)]
        moe_in = [sem(f"moe_in{i}") for i in range(RING)]
        params_in = sem("params_in")
        x_in = sem("x_in")
        mem_in = sem("mem_in")
        zeroed = sem("zeroed")
        const_ok = sem("const_ok")
        wqk_in = sem("wqk_in")
        layer_in = sem("layer_in")
        cache_in = sem("cache_in")
        stored = sem("stored")
        y_stored = sem("y_stored")
        work_zeroed = sem("work_zeroed")
        chunk_ready = sem("chunk_ready")
        act_emptied = sem("act_emptied")
        dve_emptied = sem("dve_emptied")
        act_step = sem("act_step")
        dve_step = sem("dve_step")
        pool_step = sem("pool_step")
        mem_normed = sem("mem_normed")
        drv_ready = sem("drv_ready")
        sp_exp = sem("sp_exp")
        lb_exp = sem("lb_exp")
        resid_done = sem("resid_done")
        squares_ready = sem("squares_ready")
        ssq_ready = sem("ssq_ready")
        rstd_ready = sem("rstd_ready")
        normed = sem("normed")
        memg_ready = sem("memg_ready")
        u_ready = sem("u_ready")
        ri_ready = sem("ri_ready")
        ri_used = sem("ri_used")
        la_ready = sem("la_ready")
        tn_ready = sem("tn_ready")
        beta2_ready = sem("beta2_ready")
        beta_ready = sem("beta_ready")
        hgf_ready = sem("hgf_ready")
        gla_pre = sem("gla_pre")
        gla_ln = sem("gla_ln")
        hg_ln = sem("hg_ln")
        e_ready = sem("e_ready")
        e_exp = sem("e_exp")
        lvl_qk = sem("lvl_qk")
        lvl_ready = sem("lvl_ready")
        lvl_taken = sem("lvl_taken")
        a_ready = sem("a_ready")
        kdec_ready = sem("kdec_ready")
        qdec_ready = sem("qdec_ready")
        kv_ready = sem("kv_ready")
        kv_taken = sem("kv_taken")
        o_ready = sem("o_ready")
        o_taken = sem("o_taken")
        osq_ready = sem("osq_ready")
        ors_ready = sem("ors_ready")
        gate_silu = sem("gate_silu")
        mix_ready = sem("mix_ready")
        sc_ready = sem("sc_ready")
        mx_ready = sem("mx_ready")
        ex_ready = sem("ex_ready")
        pr_ready = sem("pr_ready")
        gap_ready = sem("gap_ready")
        gexp_ready = sem("gexp_ready")
        msel_ready = sem("msel_ready")
        rounds_ready = sem("rounds_ready")
        htok_zero = sem("htok_zero")
        sel_ready = sem("sel_ready")
        gathered = sem("gathered")
        sel_used = sem("sel_used")
        selT_ready = sem("selT_ready")
        ring_free = sem("ring_free")
        kv_stored = sem("kv_stored")
        w_used = sem("w_used")
        hi_done = sem("hi_done")
        lo_done = sem("lo_done")
        hg_hi_done = sem("hg_hi_done")
        hg_ready = sem("hg_ready")
        silu_ready = sem("silu_ready")
        act_ready = sem("act_ready")
        a_turned = sem("a_turned")
        a_hi_done = sem("a_hi_done")
        a_split = sem("a_split")
        y_scaled = sem("y_scaled")
        scat_ready = sem("scat_ready")
        scat_added = sem("scat_added")
        small_ready = sem("small_ready")

        block = ctx.enter_context(nc.Block())
        by_feature = "(k p) n -> p k n"

        unit_last = []
        cn = {t: 0 for t, _ in PLAN}

        def last_of(tag, m):
            cn[tag] += m
            return CHUNK_NO[tag, cn[tag] - 1]

        for key, l, a, b in units:
            if key == "in":
                tag, m = {RX: ("rx", 2), RGT: ("rgt", 2), HF: ("hf", 2), HQ: ("hq", 2)}.get(a, (None, 0))
                if a == GR + 192:
                    last_of("ga", 1)
                    tag, m = "gate", 2
                elif tag is None:
                    tag, m = ("v", 3) if GV <= a < GR or HI <= a < HGT else ("gate", 2)
                unit_last.append(last_of(tag, m))
            elif key in ("wk", "wv"):
                unit_last.append(last_of("kv", 2))
            elif key == "out":
                unit_last.append(last_of("out", 1))
            elif key in ("wq", "wo"):
                unit_last.append(last_of(key, 2))
            elif key == "w1":
                unit_last.append(last_of("h1", 2))
            elif key == "w3":
                unit_last.append(last_of("h3", 2))
            else:
                unit_last.append(CHUNK_NO["dn", a])
        landed, total = [], [0] * DSLOTS
        for n, (key, l, a, b) in enumerate(units):
            total[n % DSLOTS] += 32 if key == "out" else 16
            landed.append(total[n % DSLOTS])
        DENSE_LAST = CHUNK_NO["wo", 8 * LAYERS - 1] + 1
        ATT_LAST = CHUNK_NO["ox", 8 * LAYERS - 1] + 1

        def slot(n, *dims):
            return view(ring, (n % DSLOTS) * SLOT, *dims)

        def unit_of(kind, s):
            if kind == 2:
                return 3 * s + 6 if s < STEPS - 2 else s + 2 * STEPS
            return (2 * s if s < 2 else 3 * s - 2) + kind

        of_unit = {unit_of(kind, s): (kind, s) for s in range(STEPS) for kind in range(3)}

        def moe_slot(u):
            return (u + DSLOTS) % RING

        def as_kind(base, off, kind):
            return view(base, off, 2, D) if kind == 2 else view(base, off, KD, 256)

        @block.sync
        def _(sp):
            sp.dma_start(xtok[:, 0:2, :], x_prompt[0].rearrange("(t p) d -> p t d", p=P)).then_inc(x_in, 16)
            sp.dma_start(xtok[0:TS, 2, :], x_sample[0]).then_inc(x_in, 16)
            sp.dma_start(mtok[:, :, :], mem_prompt[0].rearrange("(t p) d -> p t d", p=P)).then_inc(mem_in, 16)
            mats = {"in": w_in, "wk": xa_wk, "wv": xa_wv, "wq": xa_wq, "wo": xa_wo, "w1": ffd_w1, "w3": ffd_w3}
            qk_of = {("in", l, HF): l for l in range(LAYERS)}
            sp.wait_ge(zeroed, 1)
            for n, (key, l, a, b) in enumerate(units):
                if (key, l, a) in qk_of:
                    if l:
                        sp.wait_ge(chunk_ready, CHUNK_NO["k", 2 * l - 1] + 1)
                    for i, off in enumerate((GQ, GK)):
                        for h in range(4):
                            sp.dma_start(wqk[:, i, :, 64 * h:64 * h + DK_G],
                                         w_in[l][:, off + DK_G * h:off + DK_G * (h + 1)].rearrange(
                                             by_feature, p=P)).then_inc(wqk_in, 16)
                if n >= DSLOTS:
                    sp.wait_ge(chunk_ready, unit_last[n - DSLOTS] + 1)
                arrived = unit_in[n % DSLOTS]
                if key == "out":
                    sp.dma_start(slot(n, 10, P)[0:DV, 0:8, :],
                                 w_out[l][0:HEADS * DV, a:b].rearrange("(k p) n -> p k n", p=DV)).then_inc(arrived, 16)
                    sp.dma_start(slot(n, 10, P)[:, 8:10, :],
                                 w_out[l][HEADS * DV:, a:b].rearrange(by_feature, p=P)).then_inc(arrived, 16)
                elif key == "w2":
                    sp.dma_start(slot(n, STEPS, P),
                                 ffd_w2[0][STEPS * P * b:STEPS * P * (b + 1), P * a:P * a + P].rearrange(
                                     by_feature, p=P)).then_inc(arrived, 16)
                else:
                    sp.dma_start(slot(n, KD, b - a),
                                 mats[key][l][:, a:b].rearrange(by_feature, p=P)).then_inc(arrived, 16)
            def load(it, e, u, first=False):
                kind, s = of_unit[u]
                if u >= RING or not first:
                    sp.wait_ge(lo_done, it * UNITS_E + u - RING + 1)
                elif moe_slot(u) < DSLOTS:
                    sp.wait_ge(chunk_ready, DENSE_LAST)
                else:
                    sp.wait_ge(ring_free, 1)
                dst = as_kind(ring, moe_slot(u) * SLOT, kind)
                if kind == 2:
                    src = moe_w2[0, bass.ds(e, 1), 256 * s:256 * s + 256, :].rearrange(
                        "e (k p) n -> p (e k) n", p=P)
                else:
                    w = moe_w3 if kind else moe_w1
                    src = w[0, bass.ds(e, 1), :, 256 * s:256 * s + 256].rearrange("e (k p) n -> p (e k) n", p=P)
                sp.dma_start(dst, src).then_inc(moe_in[moe_slot(u)], 16)

            for u in range(RING):
                load(0, 0, u, True)
            sp.wait_ge(rounds_ready, 1)
            rounds = sp.value_load(nround[0:1, 0:1], min_val=1, max_val=MAXR)
            for u in range(RING, UNITS_E):
                load(0, 0, u, True)
            with sp.Fori(1, rounds * NE) as it:
                e = it & (NE - 1)
                sp.lower_val(e)
                for u in range(UNITS_E):
                    load(it, e, u)
            sp.wait_ge(dve_emptied, emptied("y", 5))
            sp.dma_start(y_prompt[0].rearrange("(t p) d -> p t d", p=P), ytok[:, 0:2, :]).then_inc(y_stored, 16)
            sp.dma_start(y_sample[0], ytok[0:TS, 2, :]).then_inc(y_stored, 16)
            sp.wait_ge(y_stored, 32)

        @block.gpsimd
        def _(pool):
            n_step = [0]

            def link(ins):
                n_step[0] += 1
                ins.then_inc(pool_step, 1)
                pool.wait_ge(pool_step, n_step[0])

            link(pool.memset(wqk[:, :, :, :], 0.0))
            pool.sem_inc(zeroed, 1)
            link(pool.memset(stage2[:, :], 0.0))
            row = 0
            for src, n in ((norm_mix, 16), (norm_xattn, 16), (norm_ffn, 16), (norm_mem, 16)):
                pool.dma_start(stage[row:row + n, :], src.rearrange("l (k p) -> (l k) p", p=P)).then_inc(params_in, 16)
                row += n
            pool.dma_start(stage[row:row + 8, :], norm_final.rearrange("(k p) -> k p", p=P)).then_inc(params_in, 16)
            row += 8
            for src in (hg_lb, rg_conv_b, rg_br, rg_bi, rg_lambda):
                pool.dma_start(stage[row:row + 4, :], src.rearrange("l (k p) -> (l k) p", p=P)).then_inc(params_in, 16)
                row += 4
            pool.dma_start(stage[row:row + 16, :],
                           rg_conv_w.rearrange("l j (k p) -> (l j k) p", p=P)).then_inc(params_in, 16)
            row += 16
            pool.dma_start(stage[row:row + 4, :],
                           state_rglru.rearrange("l b (k p) -> (l b k) p", p=P)).then_inc(params_in, 16)
            row += 4
            pool.dma_start(stage[row:row + 12, :],
                           state_conv.rearrange("l b j (k p) -> (l b j k) p", p=P)).then_inc(params_in, 16)
            pool.dma_start(stage2[0:8, 0:DV], gla_onorm.rearrange("l (h v) -> (l h) v", v=DV)).then_inc(params_in, 16)
            pool.dma_start(stage2[8:16, 0:DV], hg_onorm.rearrange("l (h v) -> (l h) v", v=DV)).then_inc(params_in, 16)
            for par_ in range(2):
                pool.dma_start(stage2[16:20, 64 * par_:64 * par_ + DK_G],
                               gla_ba.rearrange("l (g two k) -> (l g) two k", two=2, k=DK_G)[:, par_, :]
                               ).then_inc(params_in, 16)
            link(pool.memset(ones[:, :], 1.0))
            link(pool.memset(ident[:, :], 0.0))
            link(pool.affine_select(out=ident[:, :], in_=ident[:, :], compare_op=ALU.not_equal, fill=1.0, base=0,
                                    pattern=[[-1, P]], channel_multiplier=1))
            pool.sem_inc(const_ok, 1)
            link(pool.affine_select(out=tri[:, :], in_=ones[:, :], compare_op=ALU.is_gt, fill=0.0, base=0,
                                    pattern=[[1, P]], channel_multiplier=-1))
            link(pool.memset(restart[:, :], 1.0))
            link(pool.memset(restart[:, :].rearrange("p (c t) -> p c t", t=CH)[:, :, 0:1], 0.0))
            link(pool.iota(iota_c[:, :], [[1, C]], base=0, channel_multiplier=0, allow_small_or_imprecise_dtypes=True))
            link(pool.iota(iota_e[:, :, :], [[0, 3], [1, NE]], base=-NE, channel_multiplier=0,
                           allow_small_or_imprecise_dtypes=True))
            link(pool.iota(view(low, 0, CH).bitcast(I32), [[0, CH]], base=0, channel_multiplier=1))
            link(pool.iota(view(low, 64, CH).bitcast(I32), [[1, CH]], base=0, channel_multiplier=0))
            link(pool.memset(wa2[:, :, :], 0.0))
            link(pool.memset(wri[:, :, :, :], 0.0))
            link(pool.memset(s_init[:, :, :], 0.0))
            pool.sem_inc(const_ok, 1)
            pool.dma_start(router[:, :, :], moe_router[0].rearrange(by_feature, p=P)).then_inc(layer_in, 16)
            for l in range(LAYERS):
                for h in range(4):
                    pool.dma_start(wa2[:, l, 64 * h:64 * h + DK_G],
                                   gla_wa2[l][:, DK_G * h:DK_G * (h + 1)]).then_inc(layer_in, 16)
            for l in range(LAYERS):
                if l:
                    pool.wait_ge(ri_ready, l)
                    pool.wait_ge(o_ready, 8 * l)
                    pool.wait_ge(kv_taken, 9 * l)
                    pool.wait_ge(chunk_ready, CHUNK_NO["wo", 8 * l - 1] + 1)
                for i, w in enumerate((rg_wr, rg_wi)):
                    for blk in range(4):
                        r0 = 64 * (blk % 2)
                        pool.dma_start(wri[r0:r0 + 64, i, blk // 2, r0:r0 + 64], w[l, blk]).then_inc(layer_in, 16)
                for h in range(4):
                    r0 = 64 * (h % 2)
                    pool.dma_start(s_init[r0:r0 + DK_G, h // 2, :], state_gla[l, 0, h]).then_inc(layer_in, 16)
                    pool.dma_start(s_init[r0:r0 + DK_H, 2 + h // 2, :], state_hgrn[l, 0, h]).then_inc(layer_in, 16)
                link(pool.memset(a_full[:, :, :, :, :], 0.0))
                link(pool.memset(s_all[:, 0, :, :], 0.0))
                pool.sem_inc(work_zeroed, 1)
                pool.wait_ge(act_emptied, emptied("kv", 16 * l + 15))
                pool.dma_start(mem_k_p[l, 0].rearrange("(t p) h d -> p t (h d)", p=P), kp[:, :, :]).then_inc(kv_stored, 16)
                pool.dma_start(mem_v_p[l, 0].rearrange("(t p) h d -> p t (h d)", p=P), vp[:, :, :]).then_inc(kv_stored, 16)
                pool.wait_ge(o_ready, 8 * (l + 1))
                pool.dma_start(ks[:, :, :], cache_mem_k[l, 0].rearrange("(t p) h d -> p t (h d)", p=P)).then_inc(cache_in, 16)
                pool.dma_start(vs[:, :, :], cache_mem_v[l, 0].rearrange("(t p) h d -> p t (h d)", p=P)).then_inc(cache_in, 16)
                pool.wait_ge(kv_taken, 9 * (l + 1))
                for g, (go, ho) in enumerate(((gla_p, hgrn_p), (gla_s, hgrn_s))):
                    for h in range(4):
                        r0 = 64 * (h % 2)
                        pool.dma_start(go[l, 0, h], s_fin[r0:r0 + DK_G, g, h // 2, :]).then_inc(stored, 16)
                        pool.dma_start(ho[l, 0, h], s_fin[r0:r0 + DK_H, g, 2 + h // 2, :]).then_inc(stored, 16)
            pool.wait_ge(small_ready, 1)
            for (dst, a, n, pat) in ((rglru_p, 0, 4, "l b (k p) -> (l b k) p"), (rglru_s, 4, 4, "l b (k p) -> (l b k) p"),
                                     (conv_p, 8, 12, "l b j (k p) -> (l b j k) p"),
                                     (conv_s, 20, 12, "l b j (k p) -> (l b j k) p")):
                pool.dma_start(dst.rearrange(pat, p=P), stage3[a:a + n, :]).then_inc(stored, 16)
            pool.wait_ge(stored, 16 * (16 * LAYERS + 4))
            pool.wait_ge(kv_stored, 16 * 2 * LAYERS)

        @block.tensor
        def _(pe):
            state = {"c": 0, "u": 0}

            def mm(out, lhsT, rhs, first, last):
                return nc.tensor.matmul(out, lhsT, rhs, start=first, stop=last)

            def open_bank(tag):
                c = state["c"]
                assert PLAN[c][0] == tag, (c, PLAN[c], tag)
                if c >= 4:
                    who = PLAN[c - 4][1]
                    n = sum(1 for _, e in PLAN[:c - 3] if e == who)
                    pe.wait_ge(act_emptied if who == "A" else dve_emptied, n)
                return c % 4

            def close_bank(ins):
                ins.then_inc(chunk_ready, 1)
                state["c"] += 1

            def next_unit(*dims):
                n = state["u"]
                state["u"] += 1
                pe.wait_ge(unit_in[n % DSLOTS], landed[n])
                return slot(n, *dims)

            def project(tag, w, m0, m, rhs, n, kt=KD):
                b = open_bank(tag)
                for k in range(kt):
                    last = mm(ps[0:m, b, 0:n], w[:, k, m0:m0 + m], rhs[:, k, 0:n], k == 0, k == kt - 1)
                close_bank(last)

            def project_tokens(tag, w, width, act, t0, rows):
                b = open_bank(tag)
                for k in range(KD):
                    last = mm(ps[0:rows, b, 0:width], act[:, k, t0:t0 + rows], w[:, k, 0:width], k == 0, k == KD - 1)
                close_bank(last)

            def sum_squares(i):
                pe.wait_ge(squares_ready, i + 1)
                for k in range(KD):
                    last = mm(ps[:, 7, 0:T], ones[:, :], hT[:, k, :], k == 0, k == KD - 1)
                last.then_inc(ssq_ready, 1)
                pe.wait_ge(normed, i + 1)

            pe.wait_ge(const_ok, 1)
            pe.wait_ge(params_in, 16 * 17)
            b = open_bank("par")
            close_bank(nc.tensor.transpose(ps[:, b, 0:124], stage[0:124, :], ident[0:124, 0:124]))
            b = open_bank("par")
            close_bank(nc.tensor.transpose(ps[:, b, 0:20], stage2[0:20, :], ident[0:20, 0:20]))
            pe.wait_ge(x_in, 32)
            for t, (t0, rows) in enumerate(TILES):
                for g in range(2):
                    b = open_bank("x")
                    for j in range(4):
                        d = 4 * g + j
                        last = nc.tensor.transpose(ps[:, b, P * j:P * j + rows], xtok[0:rows, t, P * d:P * d + P],
                                                   ident[0:rows, 0:rows])
                    close_bank(last)
            pe.wait_ge(mem_normed, 1)
            for t in range(2):
                for g in range(2):
                    b = open_bank("mem")
                    for j in range(4):
                        d = 4 * g + j
                        last = nc.tensor.transpose(ps[:, b, P * j:P * j + P], mtok[:, t, P * d:P * d + P], ident[:, :])
                    close_bank(last)

            def level(l, idx):
                if idx >= 2:
                    pe.wait_ge(lvl_taken, 6 * l + idx - 1)
                if idx:
                    pe.wait_ge(lvl_qk, 5 * l + idx)
                kk, qq = (kl_t, ql_t) if idx else (k_t, q_t)
                b0 = 4 if idx % 2 else 6
                for c in range(NCH):
                    t0, tile, r0 = CH * c, c // 4, CH * (c % 4)
                    for h in range(HEADS):
                        p0, pr = 64 * (h % 2), h // 2
                        col = (tile * 4 + pr) * CH
                        last = mm(ps[r0:r0 + CH, b0 + h % 2, col:col + CH], kk[p0:p0 + 64, pr, t0:t0 + CH],
                                  qq[p0:p0 + 64, pr, t0:t0 + CH], True, True)
                last.then_inc(lvl_ready, 1)

            def kv_unit(j0, n):
                for j in range(j0, j0 + n):
                    if j % 2 == 0:
                        state["kvw"] = next_unit(KD, 256)
                    project_tokens("kv", state["kvw"], 256, memg, P * (j % 2), P)

            for l in range(LAYERS):
                sum_squares(3 * l)
                w = next_unit(KD, 256)
                for j in range(2):
                    project("rx", w, P * j, P, hT, T)
                w = next_unit(KD, 256)
                for j in range(2):
                    project("rgt", w, P * j, P, hT, T)
                pe.wait_ge(wqk_in, 128 * (l + 1))
                for i, tag in enumerate("qk"):
                    for j in range(2):
                        project(tag, wqk[:, i], P * j, P, hT, T)
                w = next_unit(KD, 256)
                for j in range(2):
                    project("hf", w, P * j, P, hT, T)
                pe.wait_ge(u_ready, l + 1)
                pe.wait_ge(layer_in, 16 * (9 + 16 * (l + 1)))
                for i in range(2):
                    for j in range(2):
                        last = mm(ps[:, 4 + 2 * i + j, 0:T], wri[:, i, j, :], u_t[:, j, :], True, True)
                last.then_inc(ri_ready, 1)
                w = next_unit(KD, 208)
                project("ga", w, 192, RANK, hT, T)
                for j in range(2):
                    project("gate", w, DV * j, DV, hT, T)
                w = next_unit(KD, 256)
                for j in range(2):
                    project("hq", w, P * j, P, hT, T)

                def values():
                    w_ = next_unit(KD, 192)
                    for t0, rows in TILES:
                        project_tokens("v", w_, 192, hT, t0, rows)

                def gates():
                    w_ = next_unit(KD, 192)
                    for j in range(2):
                        project("gate", w_, DV * j, DV, hT, T)

                pe.wait_ge(ri_used, l + 1)
                pe.wait_ge(act_emptied, emptied("ga", l))
                for j in range(2):
                    last = mm(ps[:, 4 + j, 0:T], wa2[:, l, P * j:P * j + P], gaT[0:RANK, :], True, True)
                last.then_inc(gla_pre, 1)
                values()
                pe.wait_ge(act_emptied, emptied("hq", 2 * l + 1))
                pe.wait_ge(hgf_ready, l + 1)
                level(l, 0)
                values()
                values()
                level(l, 1)
                values()
                level(l, 2)
                gates()
                level(l, 3)
                gates()
                level(l, 4)
                gates()
                level(l, 5)
                pe.wait_ge(memg_ready, l + 1)
                if l:
                    pe.wait_ge(stored, 16 * 16 * l)
                    pe.wait_ge(kv_stored, 16 * 2 * l)
                kv_unit(0, 5)
                pe.wait_ge(kdec_ready, l + 1)
                for t, (t0, rows) in enumerate(TILES):
                    b = open_bank("kdt")
                    for pr in range(PAIRS):
                        last = nc.tensor.transpose(ps[0:rows, b, P * pr:P * pr + P], kl_t[:, pr, t0:t0 + rows],
                                                   ident[:, :])
                    close_bank(last)
                kv_unit(5, 1)
                pe.wait_ge(act_emptied, emptied("kdt", 3 * l + 2))
                pe.wait_ge(lvl_taken, 6 * (l + 1))
                for c in range(NCH):
                    tile, r0 = c // 4, CH * (c % 4)
                    if c >= 4:
                        pe.wait_ge(kv_taken, 9 * l + c - 3)
                    for h in range(HEADS):
                        p0, pr = 64 * (h % 2), h // 2
                        last = mm(ps[p0:p0 + 64, 4 + c % 4, DV * pr:DV * pr + DV],
                                  kd_tok[r0:r0 + CH, tile, P * pr + p0:P * pr + p0 + 64],
                                  v_tok[r0:r0 + CH, tile, DV * h:DV * h + DV], True, True)
                    last.then_inc(kv_ready, 1)
                    if c in (4, 6):
                        kv_unit(6 + (c - 4), 2)
                kv_unit(10, 6)
                pe.wait_ge(kv_taken, 9 * (l + 1))
                pe.wait_ge(a_ready, l + 1)
                pe.wait_ge(qdec_ready, l + 1)
                for g in range(2):
                    if g:
                        pe.wait_ge(o_taken, 8 * l + 4)
                    for h in range(4 * g, 4 * g + 4):
                        for t, (t0, rows) in enumerate(TILES):
                            mm(ps[0:DV, 4 + h % 4, t0:t0 + rows], v_tok[0:rows, t, DV * h:DV * h + DV],
                               a_full[0:rows, t, h // 2, h % 2, 0:rows], t == 0, False)
                    for c in range(NCH):
                        for h in range(4 * g, 4 * g + 4):
                            p0, pr = 64 * (h % 2), h // 2
                            s = s_all[p0:p0 + 64, c, pr, :] if c < 8 else s_init[p0:p0 + 64, pr, :]
                            last = mm(ps[0:DV, 4 + h % 4, CH * c:CH * c + CH], s, ql_t[p0:p0 + 64, pr, CH * c:CH * c + CH],
                                      False, c == NCH - 1)
                            if c == NCH - 1:
                                last.then_inc(o_ready, 1)
                for h in range(HEADS):
                    pe.wait_ge(osq_ready, 8 * l + h + 1)
                    b = open_bank("oss")
                    close_bank(mm(ps[0:DV, b, 0:T], ones[0:DV, 0:DV], osq[0:DV, h, :], True, True))
                pe.wait_ge(mix_ready, l + 1)
                for d in range(KD):
                    w = next_unit(10, P)
                    b = open_bank("out")
                    for h in range(HEADS):
                        mm(ps[:, b, 0:T], w[0:DV, h, :], o_t[0:DV, h, :], h == 0, False)
                    for j in range(2):
                        last = mm(ps[:, b, 0:T], w[:, 8 + j, :], la[:, j, :], False, j == 1)
                    close_bank(last)
                sum_squares(3 * l + 1)
                for i in range(4):
                    w = next_unit(KD, 256)
                    for j in range(2):
                        project("wq", w, P * j, P, hT, T)
                for g in range(2):
                    if g:
                        pe.wait_ge(cache_in, 32 * (l + 1))
                    for t in range(2):
                        for q4 in range(2):
                            b = open_bank("kt")
                            for j in range(4):
                                d = 4 * q4 + j
                                last = nc.tensor.transpose(ps[:, b, P * j:P * j + P],
                                                           (ks if g else kp)[:, t, P * d:P * d + P], ident[:, :])
                            close_bank(last)
                pe.wait_ge(act_emptied, emptied("wq", 8 * l + 7))
                pe.wait_ge(dve_emptied, emptied("kt", 8 * l + 7))

                def scores(t):
                    t0, rows = TILES[t]
                    if t == 2:
                        pe.wait_ge(ex_ready, 3 * l + 1)
                    keys = kts if t == 2 else ktp
                    for h in range(4):
                        bank = (6 if t == 1 else 4) + h // 2
                        for j in range(2):
                            last = mm(ps[0:rows, bank, MEM * (h % 2):MEM * (h % 2) + MEM], qx[:, 2 * h + j, t0:t0 + rows],
                                      keys[:, 2 * h + j, :], j == 0, j == 1)
                    last.then_inc(sc_ready, 1)

                def turn_probs(t):
                    t0, rows = TILES[t]
                    pe.wait_ge(pr_ready, 3 * l + t + 1)
                    for g in range(2):
                        b = open_bank("pt")
                        for j in range(4):
                            h, m = 2 * g + j // 2, j % 2
                            last = nc.tensor.transpose(ps[:, b, P * j:P * j + rows],
                                                       prob[0:rows, t % 2, h, P * m:P * m + P], ident[0:rows, 0:rows])
                        close_bank(last)

                scores(0)
                scores(1)
                turn_probs(0)
                scores(2)
                turn_probs(1)
                turn_probs(2)
                pe.wait_ge(act_emptied, emptied("pt", 6 * l + 5))
                for d in range(KD):
                    b = open_bank("ox")
                    h = d // 2
                    for m in range(2):
                        mm(ps[:, b, 0:TP], vp[:, m, P * d:P * d + P], pt[:, 2 * h + m, 0:TP], m == 0, m == 1)
                    for m in range(2):
                        last = mm(ps[:, b, TP:T], vs[:, m, P * d:P * d + P], pt[:, 2 * h + m, TP:T], m == 0, m == 1)
                    close_bank(last)
                pe.wait_ge(act_emptied, emptied("ox", 8 * l + 7))
                if l == LAYERS - 1:
                    pe.wait_ge(chunk_ready, ATT_LAST)
                    pe.sem_inc(ring_free, 1)
                for i in range(4):
                    w = next_unit(KD, 256)
                    for j in range(2):
                        project("wo", w, P * j, P, hT, T)
                sum_squares(3 * l + 2)
                if l == 0:
                    for s in range(STEPS):
                        w1, w3 = next_unit(KD, 256), next_unit(KD, 256)
                        for j in range(2):
                            project("h1", w1, P * j, P, hT, T)
                            project("h3", w3, P * j, P, hT, T)
                    pe.wait_ge(dve_emptied, emptied("h3", FT - 1))
                    for d in range(KD):
                        b = open_bank("dn")
                        for half in range(2):
                            w = next_unit(STEPS, P)
                            for f in range(STEPS):
                                last = mm(ps[:, b, 0:T], w[:, f, :], act_t[:, STEPS * half + f, :],
                                          half == 0 and f == 0, half == 1 and f == STEPS - 1)
                        close_bank(last)

            for t, (t0, rows) in enumerate(TILES):
                for g in range(2):
                    b = open_bank("htok")
                    for j in range(4):
                        last = nc.tensor.transpose(ps[0:rows, b, P * j:P * j + P], hT[:, 4 * g + j, t0:t0 + rows],
                                                   ident[:, :])
                    close_bank(last)
            b = open_bank("lg")
            for t, (t0, rows) in enumerate(TILES):
                for k in range(KD):
                    last = mm(ps[0:rows, b, NE * t:NE * t + NE], hT[:, k, t0:t0 + rows], router[:, k, :], k == 0, k == KD - 1)
            close_bank(last)
            pe.wait_ge(chunk_ready, CHUNK_NO["lg", 0] + 1)
            pe.sem_inc(w_used, SPLITS)
            pe.wait_ge(msel_ready, 1)
            b = open_bank("rank")
            for t in range(3):
                for t2 in range(t + 1):
                    mm(ps[:, b, NE * t:NE * t + NE], tri[:, :] if t2 == t else ones[:, :], msel[:, t2, :], t2 == 0, t2 == t)
            for t2 in range(3):
                last = mm(ps[:, b, 3 * NE:4 * NE], ones[:, :], msel[:, t2, :], t2 == 0, t2 == 2)
            close_bank(last)
            pe.wait_ge(rounds_ready, 1)
            pe.wait_ge(act_emptied, emptied("htok", 5))
            rounds = pe.value_load(nround[0:1, 0:1], min_val=1, max_val=MAXR)

            def gather(n):
                pe.wait_ge(sel_ready, n)
                for d in range(KD):
                    out = ps[:, 5, C * d:C * d + C] if d < 5 else ps[:, 7, C * (d - 5):C * (d - 5) + C]
                    for t in range(3):
                        last = mm(out, htok[:, t, P * d:P * d + P], sel[:, t, :], t == 0, t == 2)
                last.then_inc(gathered, 1)

            def scatter(n):
                pe.wait_ge(y_scaled, n + 1)
                for d in range(KD):
                    if d >= 2:
                        pe.wait_ge(scat_added, n * KD + d - 1)
                    mm(ps[:, 6 + d % 2, 0:T], y_sb[0:C, P * d:P * d + P], selT[0:C, :], True, True).then_inc(scat_ready, 1)

            def split_mm(out, xh, xl, wh, wl, first, last):
                mm(out, xh, wh, first, False)
                mm(out, xh, wl, False, False)
                return mm(out, xl, wh, False, last)

            gather(1)
            with pe.Fori(0, rounds * NE) as it:
                def parts(kind, s):
                    u = unit_of(kind, s)
                    pe.wait_ge(lo_done, it * UNITS_E + u + 1)
                    off = (u % SPLITS) * SLOT
                    return as_kind(w_hi, off, kind), as_kind(w_lo, off, kind)

                def up(s):
                    for kind in range(2):
                        wh, wl = parts(kind, s)
                        for k in range(KD):
                            last_ = split_mm(ps[0:C, s % 2, 256 * kind:256 * kind + 256], hg_hi[:, k, :], hg_lo[:, k, :],
                                             wh[:, k, :], wl[:, k, :], k == 0, k == KD - 1)
                        last_.then_inc(w_used, 1)

                def turn(s):
                    pe.wait_ge(act_ready, it * STEPS + s + 1)
                    if s:
                        pe.wait_ge(a_split, it * STEPS + s)
                    for j in range(2):
                        last_ = nc.tensor.transpose(ps[:, 4, C * j:C * j + C], a_tok[0:C, s % 2, P * j:P * j + P],
                                                    ident[0:C, 0:C])
                    last_.then_inc(a_turned, 1)

                def down(s):
                    pe.wait_ge(a_split, it * STEPS + s + 1)
                    wh, wl = parts(2, s)
                    for j in range(2):
                        for half in range(2):
                            cols_ = slice(512 * half, 512 * half + 512)
                            last_ = split_mm(ps[0:C, 2 + half, :], a_hi[:, s % 2, j, :], a_lo[:, s % 2, j, :],
                                             wh[:, j, cols_], wl[:, j, cols_], s == 0 and j == 0,
                                             s == STEPS - 1 and j == 1)
                    last_.then_inc(w_used, 1)

                pe.wait_ge(hg_ready, it + 1)
                up(0)
                scatter(it)
                pe.wait_ge(scat_added, it * KD + KD)
                for t in range(3):
                    nc.tensor.transpose(ps[0:C, 6, P * t:P * t + P], sel[:, t, :], ident[:, :])
                for t in range(3):
                    last = mm(ps[0:C, 6, 384:385], sel[:, t, :], gcol[:, t:t + 1], t == 0, t == 2)
                last.then_inc(sel_used, 1)
                for s in range(1, STEPS):
                    up(s)
                    turn(s - 1)
                    if s >= 2:
                        down(s - 2)
                turn(STEPS - 1)
                gather(it + 2)
                down(STEPS - 2)
                down(STEPS - 1)
            scatter(rounds * NE)

            sum_squares(3 * LAYERS)
            for t, (t0, rows) in enumerate(TILES):
                for g in range(2):
                    b = open_bank("y")
                    for j in range(4):
                        last = nc.tensor.transpose(ps[0:rows, b, P * j:P * j + P], hT[:, 4 * g + j, t0:t0 + rows],
                                                   ident[:, :])
                    close_bank(last)
            b = open_bank("small")
            close_bank(nc.tensor.transpose(ps[0:32, b, 0:P], small[:, :], ident[:, :]))

        @block.scalar
        def _(act):
            st = {"c": 0, "n": 0, "s": 0}

            def link(ins):
                st["s"] += 1
                ins.then_inc(act_step, 1)
                act.wait_ge(act_step, st["s"])

            def take(tag):
                while PLAN[st["c"]][1] != "A":
                    st["c"] += 1
                assert PLAN[st["c"]][0] == tag, (PLAN[st["c"]], tag)
                c = st["c"]
                act.wait_ge(chunk_ready, c + 1)
                st["c"] += 1
                return c % 4

            def f(out, in_, func, **kw):
                return nc.scalar.activation(out, in_, func, **kw)

            def norm(i):
                act.wait_ge(resid_done, i + 1)
                f(hT[:, :, :], xT[:, :, :], ACT.Square).then_inc(squares_ready, 1)
                act.wait_ge(ssq_ready, i + 1)
                link(f(rstd[:, :], ps[:, 7, 0:T], ACT.Ln, scale=1.0 / D, bias=epsc[:, 0:1]))
                f(rstd[:, :], rstd[:, :], ACT.Exp, scale=-0.5).then_inc(rstd_ready, 1)

            act.wait_ge(mem_in, 16)
            act.wait_ge(drv_ready, 1)
            for t in range(2):
                link(f(msq[:, :], mtok[:, t, :], ACT.Square, accum_out=drv[:, v_ms + t:v_ms + t + 1]))
            link(f(drv[:, v_ms:v_ms + 2], drv[:, v_ms:v_ms + 2], ACT.Ln, scale=1.0 / D, bias=epsc[:, 0:1]))
            link(f(drv[:, v_ms:v_ms + 2], drv[:, v_ms:v_ms + 2], ACT.Exp, scale=-0.5))
            for t in range(2):
                link(f(mtok[:, t, :], mtok[:, t, :], ACT.Copy, scale=drv[:, v_ms + t:v_ms + t + 1]))
            act.sem_inc(mem_normed, 1)
            for t in range(2):
                for g in range(2):
                    b = take("mem")
                    f(memT[:, 4 * g:4 * g + 4, P * t:P * t + P],
                      ps[:, b, :].rearrange("p (j m) -> p j m", m=P), ACT.Copy).then_inc(act_emptied, 1)
            act.wait_ge(drv_ready, 2)
            f(drv[:, 32:36], drv[:, 32:36], ACT.Exp).then_inc(lb_exp, 1)
            f(drv[:, 36:40], drv[:, 36:40], ACT.Exp, scale=-1.0).then_inc(sp_exp, 1)

            for l in range(LAYERS):
                norm(3 * l)
                for j in range(2):
                    b = take("rx")
                    if l:
                        act.wait_ge(qdec_ready, l)
                    f(xc[:, j, 3:3 + TP], ps[:, b, 0:TP], ACT.Copy)
                    f(xc[:, j, 6 + TP:6 + TP + TS], ps[:, b, TP:T], ACT.Copy).then_inc(act_emptied, 1)
                for j in range(2):
                    b = take("rgt")
                    f(gb[:, j, :], ps[:, b, 0:T], ACT.Gelu_apprx_tanh).then_inc(act_emptied, 1)
                for j in range(2):
                    b = take("q")
                    f(q_t[:, j, :], ps[:, b, 0:T], ACT.Copy, scale=float(DK_G) ** -0.5).then_inc(act_emptied, 1)
                for j in range(2):
                    b = take("k")
                    f(k_t[:, j, :], ps[:, b, 0:T], ACT.Copy).then_inc(act_emptied, 1)
                for j in range(2):
                    b = take("hf")
                    f(e_t[:, 2 + j, :], ps[:, b, 0:T], ACT.Tanh, scale=0.5).then_inc(act_emptied, 1)
                act.wait_ge(ri_ready, l + 1)
                for i, dst in enumerate((la, it_)):
                    for j in range(2):
                        ins = f(dst[:, j, :], ps[:, 4 + 2 * i + j, 0:T], ACT.Tanh, scale=0.5,
                                bias=drv[:, (v_br, v_bi)[i] + 2 * l + j:(v_br, v_bi)[i] + 2 * l + j + 1])
                ins.then_inc(ri_used, 1)
                b = take("ga")
                f(gaT[0:RANK, :], ps[0:RANK, b, 0:T], ACT.Copy).then_inc(act_emptied, 1)

                def gate_copy(h):
                    b_ = take("gate")
                    f(gate[0:DV, h, :], ps[0:DV, b_, 0:T], ACT.Copy).then_inc(act_emptied, 1)

                gate_copy(2)
                gate_copy(3)
                for j in range(2):
                    b = take("hq")
                    f(q_t[:, 2 + j, :], ps[:, b, 0:T], ACT.Silu).then_inc(act_emptied, 1)
                act.wait_ge(la_ready, l + 1)
                f(tn[:, :, :], la[:, :, :], ACT.Tanh, scale=-1.0).then_inc(tn_ready, 1)

                def value_copy(n):
                    for t, (t0, rows) in enumerate(TILES):
                        b_ = take("v")
                        f(v_tok[0:rows, t, 192 * n:192 * n + 192], ps[0:rows, b_, 0:192], ACT.Copy).then_inc(act_emptied, 1)

                def kv_copy(j0, n):
                    for j in range(j0, j0 + n):
                        b_ = take("kv")
                        dst = kp if j < 8 else vp
                        o = 256 * (j % 8 // 2)
                        f(dst[:, j % 2, o:o + 256], ps[:, b_, 0:256], ACT.Copy).then_inc(act_emptied, 1)

                value_copy(0)
                act.wait_ge(gla_pre, l + 1)
                act.wait_ge(hgf_ready, l + 1)
                for j in range(2):
                    ins = f(e_t[:, j, :], ps[:, 4 + j, 0:T], ACT.Abs, bias=par2[:, 16 + 2 * l + j:17 + 2 * l + j])
                link(ins)
                link(f(e_t[:, 0:2, :], e_t[:, 0:2, :], ACT.Exp, scale=-1.0))
                f(e_t[:, 0:2, :], e_t[:, 0:2, :], ACT.Ln, bias=1.0).then_inc(gla_ln, 1)
                f(kl_t[:, 2:4, :], ql_t[:, 2:4, :], ACT.Ln).then_inc(hg_ln, 1)
                act.wait_ge(tn_ready, l + 1)
                f(la[:, :, :], la[:, :, :], ACT.Exp).then_inc(beta_ready, 1)
                value_copy(1)
                act.wait_ge(beta2_ready, l + 1)
                link(f(tn[:, :, :], tn[:, :, :], ACT.Ln))
                f(tn[:, :, :], tn[:, :, :], ACT.Exp, scale=0.5).then_inc(beta_ready, 1)
                value_copy(2)

                def level_exp(i):
                    act.wait_ge(e_ready, 6 * l + i + 1)
                    f(e_t[:, :, :], e_t[:, :, :], ACT.Exp).then_inc(e_exp, 1)

                level_exp(0)
                value_copy(3)
                level_exp(1)
                gate_copy(0)
                gate_copy(1)
                level_exp(2)
                gate_copy(4)
                gate_copy(5)
                level_exp(3)
                gate_copy(6)
                gate_copy(7)
                level_exp(4)
                if l:
                    act.wait_ge(kv_stored, 16 * 2 * l)
                kv_copy(0, 5)
                level_exp(5)
                act.wait_ge(kdec_ready, l + 1)
                f(e_t[:, :, :], b_t[:, :, :], ACT.Exp).then_inc(e_exp, 1)
                for t, (t0, rows) in enumerate(TILES):
                    b = take("kdt")
                    f(kd_tok[0:rows, t, :], ps[0:rows, b, :], ACT.Copy).then_inc(act_emptied, 1)
                kv_copy(5, 5)
                act.wait_ge(lvl_taken, 6 * (l + 1))
                act.wait_ge(work_zeroed, l + 1)
                for blk in range(4):
                    r0 = CH * blk
                    nt = 3 if blk == 0 else 2
                    for pr in range(2):
                        for t in range(nt):
                            ins = f(a_full[r0:r0 + CH, t, :, pr, r0:r0 + CH], a_comp[r0:r0 + CH, pr, t, :, :], ACT.Copy)
                ins.then_inc(a_ready, 1)
                kv_copy(10, 6)
                for h in range(HEADS):
                    act.wait_ge(o_ready, 8 * l + h + 1)
                    if h == 0:
                        act.wait_ge(a_ready, l + 1)
                        act.wait_ge(qdec_ready, l + 1)
                    f(osq[0:DV, h, :], ps[0:DV, 4 + h % 4, 0:T], ACT.Square).then_inc(osq_ready, 1)
                    f(o_t[0:DV, h, :], ps[0:DV, 4 + h % 4, 0:T], ACT.Copy).then_inc(o_taken, 1)
                for h in range(HEADS):
                    b = take("oss")
                    f(osq[0:DV, h, :], ps[0:DV, b, 0:T], ACT.Ln, scale=1.0 / DV, bias=epsc[0:DV, 0:1]).then_inc(act_emptied, 1)
                act.wait_ge(act_emptied, emptied("oss", 8 * l + 7))
                f(osq[0:DV, :, :], osq[0:DV, :, :], ACT.Exp, scale=-0.5).then_inc(ors_ready, 1)
                f(gate[0:DV, :, :], gate[0:DV, :, :], ACT.Silu).then_inc(gate_silu, 1)
                norm(3 * l + 1)
                act.wait_ge(mix_ready, l + 1)
                for j in range(8):
                    b = take("wq")
                    f(qx[:, j, :], ps[:, b, 0:T], ACT.Copy).then_inc(act_emptied, 1)

                def exps(t):
                    rows = TILES[t][1]
                    act.wait_ge(mx_ready, 3 * l + t + 1)
                    if t == 2:
                        act.wait_ge(chunk_ready, CHUNK_NO["pt", 6 * l + 1] + 1)
                    for h in range(4):
                        bank = (6 if t == 1 else 4) + h // 2
                        ins_ = f(prob[0:rows, t % 2, h, :], ps[0:rows, bank, MEM * (h % 2):MEM * (h % 2) + MEM], ACT.Exp,
                                 scale=1.0 / 16, bias=att[0:rows, t % 2, 4 + h:5 + h],
                                 accum_out=att[0:rows, t % 2, 8 + h:9 + h])
                    ins_.then_inc(ex_ready, 1)

                def turn_copy(t):
                    t0, rows = TILES[t]
                    for g in range(2):
                        b_ = take("pt")
                        f(pt[:, 4 * g:4 * g + 4, t0:t0 + rows],
                          ps[:, b_, :].rearrange("p (j m) -> p j m", m=P)[:, :, 0:rows], ACT.Copy).then_inc(act_emptied, 1)

                exps(0)
                exps(1)
                turn_copy(0)
                exps(2)
                turn_copy(1)
                turn_copy(2)
                for d in range(KD):
                    b = take("ox")
                    f(hT[:, d, :], ps[:, b, 0:T], ACT.Copy).then_inc(act_emptied, 1)
                norm(3 * l + 2)
                if l == 0:
                    for i in range(FT):
                        b = take("h1")
                        if i >= 2:
                            act.wait_ge(dve_emptied, emptied("h3", i - 2))
                        f(sil0[:, i % 2, :], ps[:, b, 0:T], ACT.Silu).then_inc(act_emptied, 1)

            act.wait_ge(htok_zero, 1)
            for t, (t0, rows) in enumerate(TILES):
                for g in range(2):
                    b = take("htok")
                    f(htok[0:rows, t, 512 * g:512 * g + 512], ps[0:rows, b, :], ACT.Copy).then_inc(act_emptied, 1)
            act.wait_ge(gap_ready, 1)
            f(cols[:, 6:9], cols[:, 6:9], ACT.Exp).then_inc(gexp_ready, 1)
            act.wait_ge(rounds_ready, 1)
            rounds = act.value_load(nround[0:1, 0:1], min_val=1, max_val=MAXR)
            act.wait_ge(kv_stored, 16 * 2 * LAYERS)

            def gather_hi(n):
                act.wait_ge(gathered, n)
                f(hg_hi[:, 0:5, :], ps[:, 5, 0:5 * C].rearrange("p (j m) -> p j m", m=C), ACT.Copy)
                f(hg_hi[:, 5:8, :], ps[:, 7, 0:3 * C].rearrange("p (j m) -> p j m", m=C), ACT.Copy).then_inc(hg_hi_done, 1)

            gather_hi(1)
            with act.Fori(0, rounds * NE) as it:
                def weight_hi(u):
                    act.wait_ge(moe_in[moe_slot(u)], it * (16 * UNITS_E // RING) + 16 * (u // RING + 1))
                    act.wait_ge(w_used, it * UNITS_E + u + 1)
                    f(view(w_hi, (u % SPLITS) * SLOT, SLOT), view(ring, moe_slot(u) * SLOT, SLOT),
                      ACT.Copy).then_inc(hi_done, 1)

                def silu(s):
                    act.wait_ge(w_used, it * UNITS_E + unit_of(1, s) + 1 + SPLITS)
                    f(sil[0:C, s % 2, :], ps[0:C, s % 2, 0:256], ACT.Silu).then_inc(silu_ready, 1)

                def act_hi(s):
                    act.wait_ge(a_turned, it * STEPS + s + 1)
                    f(a_hi[:, s % 2, :, :], ps[:, 4, 0:2 * C].rearrange("p (j m) -> p j m", m=C),
                      ACT.Copy).then_inc(a_hi_done, 1)

                weight_hi(0)
                weight_hi(1)
                weight_hi(2)
                weight_hi(3)
                silu(0)
                weight_hi(4)
                act.wait_ge(sel_used, it + 1)
                f(selT[0:C, :], ps[0:C, 6, 0:T], ACT.Copy).then_inc(selT_ready, 1)
                weight_hi(5)
                silu(1)
                weight_hi(6)
                act_hi(0)
                for s in range(2, STEPS - 1):
                    weight_hi(3 * s + 1)
                    silu(s)
                    weight_hi(3 * s + 2)
                    act_hi(s - 1)
                    weight_hi(3 * s + 3)
                weight_hi(UNITS_E - 2)
                silu(STEPS - 1)
                weight_hi(UNITS_E - 1)
                act_hi(STEPS - 2)
                act_hi(STEPS - 1)
                gather_hi(it + 2)
            norm(3 * LAYERS)

        @block.vector
        def _(dve):
            st = {"c": 0, "s": 0}
            V = nc.vector

            def link(ins):
                st["s"] += 1
                ins.then_inc(dve_step, 1)
                dve.wait_ge(dve_step, st["s"])

            def take(tag):
                while PLAN[st["c"]][1] != "V":
                    st["c"] += 1
                assert PLAN[st["c"]][0] == tag, (PLAN[st["c"]], tag)
                c = st["c"]
                dve.wait_ge(chunk_ready, c + 1)
                st["c"] += 1
                return c % 4

            def add_residual(tag, n):
                for d in range(KD):
                    b_ = take(tag)
                    V.tensor_tensor(xT[:, d, :], xT[:, d, :], ps[:, b_, 0:T], ALU.add).then_inc(dve_emptied, 1)
                dve.wait_ge(dve_emptied, emptied(tag, n))
                V.sem_inc(resid_done, 1)

            def norm(i, gains):
                dve.wait_ge(rstd_ready, i + 1)
                for k in range(KD):
                    ins = V.scalar_tensor_tensor(out=hT[:, k, :], in0=xT[:, k, :], scalar=par[:, gains + k:gains + k + 1],
                                                 in1=rstd[:, :], op0=ALU.mult, op1=ALU.mult)
                ins.then_inc(normed, 1)

            V.memset(epsc[:, :], EPS).then_inc(drv_ready, 1)
            dve.wait_ge(const_ok, 2)
            s_i, t_i = view(low, 0, CH).bitcast(I32), view(low, 64, CH).bitcast(I32)
            x_i, g_f = view(low, 128, CH).bitcast(I32), view(low, 192, CH)
            m_f = view(low, 256, CH)
            link(V.tensor_scalar(s_i, s_i, CH - 1, None, ALU.bitwise_and))
            link(V.tensor_tensor(x_i, s_i, t_i, ALU.bitwise_xor))
            link(V.tensor_tensor(g_f, t_i, s_i, ALU.is_gt))
            link(V.tensor_scalar(masks[:, 0, :], x_i, 0.0, None, ALU.is_equal))
            for i, h in enumerate(LEVELS):
                link(V.scalar_tensor_tensor(out=m_f, in0=x_i, scalar=float(h), in1=g_f, op0=ALU.is_ge, op1=ALU.mult))
                link(V.scalar_tensor_tensor(out=masks[:, 1 + i, :], in0=x_i, scalar=float(2 * h), in1=m_f,
                                            op0=ALU.is_lt, op1=ALU.mult))
            b = take("par")
            link(V.tensor_copy(par[:, :], ps[:, b, 0:124]))
            V.sem_inc(dve_emptied, 1)
            b = take("par")
            link(V.tensor_copy(par2[:, :], ps[:, b, 0:20]))
            V.sem_inc(dve_emptied, 1)
            lb = par[:, c_lb:c_lb + 4]
            lam = par[:, c_lam:c_lam + 4]
            link(V.tensor_tensor(drv[:, 40:42], lb[:, 0:2], lb[:, 2:4], ALU.max))
            link(V.tensor_tensor(drv[:, 32:34], lb[:, 0:2], drv[:, 40:42], ALU.subtract))
            link(V.tensor_tensor(drv[:, 34:36], lb[:, 2:4], drv[:, 40:42], ALU.subtract))
            link(V.tensor_scalar(drv[:, 40:44], lam, -1.0, None, ALU.mult))
            link(V.tensor_tensor(drv[:, 36:40], lam, drv[:, 40:44], ALU.max))
            link(V.tensor_scalar(drv[:, 44:48], drv[:, 40:44], 0.0, None, ALU.max))
            V.sem_inc(drv_ready, 1)
            for t, (t0, rows) in enumerate(TILES):
                for g in range(2):
                    b = take("x")
                    V.tensor_copy(xT[:, 4 * g:4 * g + 4, t0:t0 + rows],
                                  ps[:, b, :].rearrange("p (j m) -> p j m", m=P)[:, :, 0:rows]).then_inc(dve_emptied, 1)
            dve.wait_ge(dve_emptied, emptied("x", 5))
            V.sem_inc(resid_done, 1)
            dve.wait_ge(lb_exp, 1)
            dve.wait_ge(sp_exp, 1)
            link(V.tensor_tensor(drv[:, 40:42], drv[:, 32:34], drv[:, 34:36], ALU.add))
            link(V.reciprocal(drv[:, 40:42], drv[:, 40:42]))
            link(V.tensor_tensor(drv[:, 34:36], drv[:, 34:36], drv[:, 40:42], ALU.mult))
            link(V.memset(drv[:, 32:34], 0.0))
            link(V.tensor_scalar(drv[:, v_kA:v_kA + 4], drv[:, 32:36], 0.5, -0.5, ALU.mult, ALU.add))
            link(V.tensor_scalar(drv[:, v_kB:v_kB + 4], drv[:, 32:36], -0.5, 0.5, ALU.mult, ALU.add))
            link(V.tensor_scalar(drv[:, v_fb:v_fb + 4], drv[:, 32:36], 0.5, 0.5, ALU.mult, ALU.add))
            e_c, s_c, s2_c, p_c = drv[:, 36:40], drv[:, 48:52], drv[:, 52:56], drv[:, 56:60]
            link(V.tensor_scalar(s_c, e_c, 2.0, None, ALU.add))
            link(V.reciprocal(s_c, s_c))
            link(V.tensor_tensor(s_c, s_c, e_c, ALU.mult))
            link(V.tensor_tensor(s2_c, s_c, s_c, ALU.mult))
            link(V.tensor_scalar(p_c, s2_c, 1.0 / 17, 1.0 / 15, ALU.mult, ALU.add))
            for n in (13, 11, 9, 7, 5, 3, 1):
                link(V.tensor_tensor(p_c, p_c, s2_c, ALU.mult))
                link(V.tensor_scalar(p_c, p_c, 1.0 / n, None, ALU.add))
            link(V.tensor_tensor(p_c, p_c, s_c, ALU.mult))
            link(V.tensor_scalar(p_c, p_c, 2.0, None, ALU.mult))
            link(V.tensor_tensor(p_c, p_c, drv[:, 44:48], ALU.add))
            link(V.tensor_scalar(drv[:, v_sp:v_sp + 4], p_c, -4.0, None, ALU.mult))
            link(V.tensor_scalar(drv[:, v_br:v_br + 8], par[:, c_br:c_br + 8], 0.5, None, ALU.mult))
            for l in range(LAYERS):
                norm(3 * l, c_mix + 8 * l)
                if l == 0:
                    dve.wait_ge(act_emptied, emptied("mem", 3))
                for k in range(KD):
                    ins = V.tensor_scalar(memg[:, k, :], memT[:, k, :], par[:, c_mem + 8 * l + k:c_mem + 8 * l + k + 1],
                                          None, ALU.mult)
                ins.then_inc(memg_ready, 1)
                V.memset(xc[:, :, 0:3], 0.0)
                link(V.tensor_copy(xc[:, :, 3 + TP:6 + TP],
                                   par[:, c_c0 + 6 * l:c_c0 + 6 * l + 6].rearrange("p (j k) -> p k j", k=2)))
                dve.wait_ge(act_emptied, emptied("rx", 2 * l + 1))
                for j in range(2):
                    cw = c_cw + 8 * l + j
                    for x0, u0, n in ((0, 0, TP), (3 + TP, TP, TS)):
                        V.tensor_scalar(u_t[:, j, u0:u0 + n], xc[:, j, x0:x0 + n], par[:, cw:cw + 1],
                                        par[:, c_cb + 2 * l + j:c_cb + 2 * l + j + 1], ALU.mult, ALU.add
                                        ).then_inc(dve_step, 1)
                        st["s"] += 1
                for i in range(1, CONV):
                    dve.wait_ge(dve_step, st["s"])
                    for j in range(2):
                        cw = c_cw + 8 * l + 2 * i + j
                        for x0, u0, n in ((0, 0, TP), (3 + TP, TP, TS)):
                            V.scalar_tensor_tensor(out=u_t[:, j, u0:u0 + n], in0=xc[:, j, x0 + i:x0 + i + n],
                                                   scalar=par[:, cw:cw + 1], in1=u_t[:, j, u0:u0 + n],
                                                   op0=ALU.mult, op1=ALU.add).then_inc(dve_step, 1)
                            st["s"] += 1
                dve.wait_ge(dve_step, st["s"])
                V.sem_inc(u_ready, 1)
                for g, x0 in enumerate((TP, 3 + TP + TS)):
                    V.tensor_copy(small[:, 8 + 12 * g + 6 * l:14 + 12 * g + 6 * l].rearrange("p (j k) -> p k j", k=2),
                                  xc[:, :, x0:x0 + 3])
                dve.wait_ge(act_emptied, emptied("hf", 2 * l + 1))
                for j in range(2):
                    c_ = 2 * l + j
                    V.tensor_scalar(k_t[:, 2 + j, :], e_t[:, 2 + j, :], drv[:, v_kA + c_:v_kA + c_ + 1],
                                    drv[:, v_kB + c_:v_kB + c_ + 1], ALU.mult, ALU.add)
                    link(V.tensor_scalar(ql_t[:, 2 + j, :], e_t[:, 2 + j, :], drv[:, v_kB + c_:v_kB + c_ + 1],
                                         drv[:, v_fb + c_:v_fb + c_ + 1], ALU.mult, ALU.add))
                V.tensor_scalar(ql_t[:, 2:4, :], ql_t[:, 2:4, :], 1e-19, None, ALU.max).then_inc(hgf_ready, 1)
                dve.wait_ge(ri_used, l + 1)
                for j in range(2):
                    c_ = v_sp + 2 * l + j
                    ins = V.tensor_scalar(la[:, j, :], la[:, j, :], drv[:, c_:c_ + 1], drv[:, c_:c_ + 1], ALU.mult, ALU.add)
                ins.then_inc(la_ready, 1)
                link(V.tensor_scalar(it_[:, :, :], it_[:, :, :], 0.5, 0.5, ALU.mult, ALU.add))
                link(V.tensor_tensor(it_[:, :, :], it_[:, :, :], u_t[:, :, :], ALU.mult))
                dve.wait_ge(gla_ln, l + 1)
                for j in range(2):
                    c_ = 16 + 2 * l + j
                    ins = V.tensor_scalar(kl_t[:, j, :], ps[:, 4 + j, 0:T], par2[:, c_:c_ + 1], 0.0, ALU.add, ALU.min)
                link(ins)
                link(V.tensor_tensor(kl_t[:, 0:2, :], kl_t[:, 0:2, :], e_t[:, 0:2, :], ALU.subtract))
                link(V.tensor_scalar(kl_t[:, 0:2, :], kl_t[:, 0:2, :], 1.0 / 16, None, ALU.mult))
                dve.wait_ge(hg_ln, l + 1)
                for pr in range(PAIRS):
                    ins = V.tensor_tensor_scan(out=b_t[:, pr, :], data0=restart[:, :], data1=kl_t[:, pr, :], initial=0.0,
                                               op0=ALU.mult, op1=ALU.add)
                link(ins)
                link(V.memset(ql_t[:, 0:2, :], 0.0))

                def blocks(x, s):
                    return x.rearrange("p a (n s) -> p (a n) s", s=s)

                def level_e(i):
                    h = LEVELS[i]
                    bv, ev = blocks(b_t, 2 * h), blocks(e_t, 2 * h)
                    n = PAIRS * T // (2 * h)
                    mid = bv[:, :, h - 1:h].to_broadcast([P, n, h])
                    V.tensor_tensor(ev[:, :, 0:h], mid, bv[:, :, 0:h], ALU.subtract)
                    V.tensor_tensor(ev[:, :, h:2 * h], bv[:, :, h:2 * h], mid, ALU.subtract).then_inc(e_ready, 1)

                def level_qk(i):
                    h = LEVELS[i]
                    dve.wait_ge(e_exp, 7 * l + i + 1)
                    if i:
                        dve.wait_ge(lvl_ready, 6 * l + i + 1)
                    ev = blocks(e_t, 2 * h)
                    V.tensor_tensor(blocks(kl_t, 2 * h)[:, :, 0:h], blocks(k_t, 2 * h)[:, :, 0:h], ev[:, :, 0:h], ALU.mult)
                    ins_ = V.tensor_tensor(blocks(ql_t, 2 * h)[:, :, h:2 * h], blocks(q_t, 2 * h)[:, :, h:2 * h],
                                           ev[:, :, h:2 * h], ALU.mult)
                    ins_.then_inc(lvl_qk, 1)
                    dve.wait_ge(lvl_qk, 5 * l + i + 1)

                def level_take(idx):
                    dve.wait_ge(lvl_ready, 6 * l + idx + 1)
                    b0 = 4 if idx % 2 else 6
                    for pr in range(2):
                        V.copy_predicated(a_comp[:, pr, 0:2, :, :].rearrange("p t g c -> p (t g) c"),
                                          masks[:, idx:idx + 1, :].to_broadcast([P, 8, CH]),
                                          ps[:, b0 + pr, 0:8 * CH].rearrange("p (g c) -> p g c", c=CH))
                        ins_ = V.copy_predicated(a_comp[0:CH, pr, 2, :, :],
                                                 masks[0:CH, idx:idx + 1, :].to_broadcast([CH, 4, CH]),
                                                 ps[0:CH, b0 + pr, 8 * CH:12 * CH].rearrange("p (g c) -> p g c", c=CH))
                    ins_.then_inc(lvl_taken, 1)
                    dve.wait_ge(lvl_taken, 6 * l + idx + 1)

                level_e(0)
                link(V.memset(a_comp[:, :, :, :, :], 0.0))
                dve.wait_ge(beta_ready, 2 * l + 1)
                link(V.tensor_tensor(u_t[:, :, :], la[:, :, :], la[:, :, :], ALU.mult))
                link(V.scalar_tensor_tensor(out=tn[:, :, :], in0=u_t[:, :, :], scalar=1.0, in1=tn[:, :, :],
                                            op0=ALU.add, op1=ALU.mult))
                V.tensor_scalar(tn[:, :, :], tn[:, :, :], 1e-12, None, ALU.max).then_inc(beta2_ready, 1)
                level_take(0)
                level_qk(0)
                level_e(1)
                dve.wait_ge(beta_ready, 2 * l + 2)
                link(V.tensor_tensor(it_[:, :, :], it_[:, :, :], tn[:, :, :], ALU.mult))
                for j in range(2):
                    V.tensor_tensor_scan(out=tn[:, j, 0:TP], data0=la[:, j, 0:TP], data1=it_[:, j, 0:TP], initial=0.0,
                                         op0=ALU.mult, op1=ALU.add)
                    h0 = c_h0 + 2 * l + j
                    ins = V.tensor_tensor_scan(out=tn[:, j, TP:T], data0=la[:, j, TP:T], data1=it_[:, j, TP:T],
                                               initial=par[:, h0:h0 + 1], op0=ALU.mult, op1=ALU.add)
                link(ins)
                for g, t_ in enumerate((TP - 1, T - 1)):
                    V.tensor_copy(small[:, 4 * g + 2 * l:4 * g + 2 * l + 2], tn[:, :, t_])
                link(V.tensor_tensor(la[:, :, :], tn[:, :, :], gb[:, :, :], ALU.mult))
                level_take(1)
                for i in range(1, 5):
                    level_qk(i)
                    if i < 4:
                        level_e(i + 1)
                    else:
                        bv, ev = blocks(b_t, CH), blocks(e_t, CH)
                        V.tensor_tensor(ev[:, :, :], bv[:, :, CH - 1:CH].to_broadcast([P, PAIRS * NCH, CH]), bv[:, :, :],
                                        ALU.subtract).then_inc(e_ready, 1)
                    level_take(i + 1)
                dve.wait_ge(e_exp, 7 * l + 6)
                V.tensor_tensor(kl_t[:, :, :], k_t[:, :, :], e_t[:, :, :], ALU.mult).then_inc(kdec_ready, 1)
                dve.wait_ge(e_exp, 7 * l + 7)
                V.tensor_tensor(ql_t[:, :, :], q_t[:, :, :], e_t[:, :, :], ALU.mult).then_inc(qdec_ready, 1)
                dve.wait_ge(work_zeroed, l + 1)
                dve.wait_ge(layer_in, 16 * (9 + 16 * (l + 1)))
                if l:
                    dve.wait_ge(stored, 16 * 16 * l)
                eb = e_t.rearrange("p a (c t) -> p a c t", t=CH)
                for c in range(NCH):
                    s_in = s_all[:, c, :, :] if c < 8 else s_init[:, :, :]
                    s_out = s_all[:, c + 1, :, :] if c < 7 else s_fin[:, c - 7, :, :]
                    link(V.tensor_tensor(s_out, s_in, eb[:, :, c, CH - 1:CH].to_broadcast([P, PAIRS, DV]), ALU.mult))
                    dve.wait_ge(kv_ready, 9 * l + c + 1)
                    V.tensor_tensor(s_out, s_out, ps[:, 4 + c % 4, 0:PAIRS * DV].rearrange("p (a v) -> p a v", v=DV),
                                    ALU.add).then_inc(kv_taken, 1)
                    dve.wait_ge(kv_taken, 9 * l + c + 1)
                dve.wait_ge(o_taken, 8 * (l + 1))
                dve.wait_ge(ors_ready, l + 1)
                for h in range(HEADS):
                    col = 4 * l + h if h < 4 else 8 + 4 * l + h - 4
                    ins = V.scalar_tensor_tensor(out=o_t[0:DV, h, :], in0=o_t[0:DV, h, :], scalar=par2[0:DV, col:col + 1],
                                                 in1=osq[0:DV, h, :], op0=ALU.mult, op1=ALU.mult)
                link(ins)
                dve.wait_ge(gate_silu, l + 1)
                V.tensor_tensor(o_t[0:DV, :, :], o_t[0:DV, :, :], gate[0:DV, :, :], ALU.mult).then_inc(mix_ready, 1)
                dve.wait_ge(mix_ready, l + 1)
                add_residual("out", 8 * l + 7)
                norm(3 * l + 1, c_xa + 8 * l)
                for g in range(2):
                    for t in range(2):
                        for q4 in range(2):
                            b = take("kt")
                            V.tensor_copy((kts if g else ktp)[:, 4 * q4:4 * q4 + 4, P * t:P * t + P],
                                          ps[:, b, :].rearrange("p (j m) -> p j m", m=P)).then_inc(dve_emptied, 1)

                def maxima(t):
                    rows = TILES[t][1]
                    dve.wait_ge(sc_ready, 3 * l + t + 1)
                    b0 = 6 if t == 1 else 4
                    link(V.tensor_reduce(att[0:rows, t % 2, 0:4],
                                         ps[0:rows, b0:b0 + 2, :].rearrange("p b (h m) -> p (b h) m", m=MEM),
                                         AX.X, ALU.max))
                    V.tensor_scalar(att[0:rows, t % 2, 4:8], att[0:rows, t % 2, 0:4], -1.0 / 16, None,
                                    ALU.mult).then_inc(mx_ready, 1)

                def divide(t):
                    rows = TILES[t][1]
                    dve.wait_ge(ex_ready, 3 * l + t + 1)
                    link(V.reciprocal(att[0:rows, t % 2, 12:16], att[0:rows, t % 2, 8:12]))
                    for h in range(4):
                        ins_ = V.tensor_scalar(prob[0:rows, t % 2, h, :], prob[0:rows, t % 2, h, :],
                                               att[0:rows, t % 2, 12 + h:13 + h], None, ALU.mult)
                    ins_.then_inc(pr_ready, 1)
                    dve.wait_ge(pr_ready, 3 * l + t + 1)

                maxima(0)
                maxima(1)
                divide(0)
                maxima(2)
                divide(1)
                divide(2)
                add_residual("wo", 8 * l + 7)
                norm(3 * l + 2, c_ff + 8 * l)
                if l == 0:
                    for i in range(FT):
                        b = take("h3")
                        dve.wait_ge(act_emptied, emptied("h1", i))
                        V.tensor_tensor(act_t[:, i, :], sil0[:, i % 2, :], ps[:, b, 0:T], ALU.mult).then_inc(dve_emptied, 1)
                    add_residual("dn", 7)

            V.memset(htok[:, 2, :], 0.0).then_inc(htok_zero, 1)
            link(V.memset(lgt[:, :, :], 0.0))
            b = take("lg")
            V.tensor_copy(lgt[:, 0:2, :], ps[:, b, 0:2 * NE].rearrange("p (t e) -> p t e", e=NE))
            link(V.tensor_copy(lgt[0:TS, 2, :], ps[0:TS, b, 2 * NE:3 * NE]))
            V.sem_inc(dve_emptied, 1)
            for i, oh in enumerate((oh1, oh2)):
                link(V.tensor_reduce(cols[:, 3 * i:3 * i + 3], lgt[:, :, :], AX.X, ALU.max))
                top = cols[:, 3 * i:3 * i + 3].rearrange("p (t e) -> p t e", e=1).to_broadcast([P, 3, NE])
                link(V.tensor_tensor(tmp8[:, :, :], lgt[:, :, :], top, ALU.is_equal))
                link(V.tensor_tensor(tmp8[:, :, :], tmp8[:, :, :], iota_e[:, :, :], ALU.mult))
                link(V.tensor_reduce(cols[:, 12:15], tmp8[:, :, :], AX.X, ALU.min))
                first = cols[:, 12:15].rearrange("p (t e) -> p t e", e=1).to_broadcast([P, 3, NE])
                link(V.tensor_tensor(oh, iota_e[:, :, :], first, ALU.is_equal))
                if i == 0:
                    link(V.scalar_tensor_tensor(out=lgt[:, :, :], in0=oh, scalar=-3e38, in1=lgt[:, :, :],
                                                op0=ALU.mult, op1=ALU.add))
            link(V.tensor_tensor(cols[:, 6:9], cols[:, 3:6], cols[:, 0:3], ALU.subtract))
            V.sem_inc(gap_ready, 1)
            link(V.tensor_tensor(msel[:, :, :], oh1, oh2, ALU.add))
            link(V.memset(msel[TS:64, 2, :], 0.0))
            link(V.memset(msel[64:P, 2, :], 0.0))
            V.sem_inc(msel_ready, 1)
            dve.wait_ge(gexp_ready, 1)
            link(V.tensor_scalar(cols[:, 9:12], cols[:, 6:9], 1.0, None, ALU.add))
            link(V.reciprocal(cols[:, 9:12], cols[:, 9:12]))
            link(V.tensor_tensor(cols[:, 6:9], cols[:, 6:9], cols[:, 9:12], ALU.mult))
            g1 = cols[:, 9:12].rearrange("p (t e) -> p t e", e=1).to_broadcast([P, 3, NE])
            g2 = cols[:, 6:9].rearrange("p (t e) -> p t e", e=1).to_broadcast([P, 3, NE])
            link(V.tensor_tensor(gd[:, :, :], oh1, g1, ALU.mult))
            link(V.tensor_tensor(tmp8[:, :, :], oh2, g2, ALU.mult))
            link(V.tensor_tensor(gd[:, :, :], gd[:, :, :], tmp8[:, :, :], ALU.add))
            b = take("rank")
            link(V.scalar_tensor_tensor(out=tmp8[:, :, :], in0=ps[:, b, 0:3 * NE].rearrange("p (t e) -> p t e", e=NE),
                                        scalar=1024.0, in1=msel[:, :, :], op0=ALU.add, op1=ALU.mult))
            for r in range(MAXR + 1):
                link(V.tensor_scalar(posr[:, :, NE * r:NE * r + NE], tmp8[:, :, :], -1024.0 - C * r, None, ALU.add))
            link(V.tensor_reduce(cols[0:1, 16:17], ps[0:1, b, 3 * NE:4 * NE], AX.X, ALU.max))
            V.sem_inc(dve_emptied, 1)
            link(V.tensor_scalar(cols[0:1, 17:18], cols[0:1, 16:17], float(C), 1.0, ALU.is_gt, ALU.add))
            link(V.tensor_scalar(cols[0:1, 18:19], cols[0:1, 16:17], float(2 * C), None, ALU.is_gt))
            link(V.tensor_tensor(cols[0:1, 19:20], cols[0:1, 17:18], cols[0:1, 18:19], ALU.add))
            link(V.tensor_copy(nround[0:1, 0:1], cols[0:1, 19:20]))
            V.sem_inc(rounds_ready, 1)
            rounds = dve.value_load(nround[0:1, 0:1], min_val=1, max_val=MAXR)
            dve.wait_ge(act_emptied, emptied("htok", 5))
            V.memset(ps[0:C, 2:4, :], 0.0)
            V.memset(gs[0:C, :], 0.0)
            link(V.memset(selT[0:C, :], 0.0))

            def gather_lo(n):
                dve.wait_ge(hg_hi_done, n)
                V.tensor_tensor(hg_lo[:, 0:5, :], ps[:, 5, 0:5 * C].rearrange("p (j m) -> p j m", m=C),
                                hg_hi[:, 0:5, :].bitcast(F32), ALU.subtract)
                V.tensor_tensor(hg_lo[:, 5:8, :], ps[:, 7, 0:3 * C].rearrange("p (j m) -> p j m", m=C),
                                hg_hi[:, 5:8, :].bitcast(F32), ALU.subtract).then_inc(hg_ready, 1)

            def scale_y(n):
                dve.wait_ge(w_used, n * UNITS_E + SPLITS)
                V.tensor_scalar(y_sb[0:C, :], ps[0:C, 2:4, :].rearrange("p b n -> p (b n)"), gs[0:C, 0:1], None,
                                ALU.mult).then_inc(y_scaled, 1)

            def add_y(n):
                for d in range(KD):
                    dve.wait_ge(scat_ready, n * KD + d + 1)
                    V.tensor_tensor(xT[:, d, :], xT[:, d, :], ps[:, 6 + d % 2, 0:T], ALU.add).then_inc(scat_added, 1)

            V.tensor_copy(gcol[:, :].rearrange("p (t e) -> p t e", e=1), gd[:, :, 0:1])
            for t in range(3):
                ins = V.tensor_scalar(sel[:, t, :], iota_c[:, :], posr[:, t, 0:1], None, ALU.is_equal)
            ins.then_inc(sel_ready, 1)
            gather_lo(1)
            with dve.Fori(0, rounds * NE) as it:
                def weight_lo(u):
                    dve.wait_ge(hi_done, it * UNITS_E + u + 1)
                    off = (u % SPLITS) * SLOT
                    V.tensor_tensor(view(w_lo, off, SLOT), view(ring, moe_slot(u) * SLOT, SLOT),
                                    view(w_hi, off, SLOT).bitcast(F32), ALU.subtract).then_inc(lo_done, 1)

                def multiply(s):
                    dve.wait_ge(silu_ready, it * STEPS + s + 1)
                    V.tensor_tensor(a_tok[0:C, s % 2, :], sil[0:C, s % 2, :], ps[0:C, s % 2, 256:512],
                                    ALU.mult).then_inc(act_ready, 1)

                def act_lo(s):
                    dve.wait_ge(a_hi_done, it * STEPS + s + 1)
                    V.tensor_tensor(a_lo[:, s % 2, :, :], ps[:, 4, 0:2 * C].rearrange("p (j m) -> p j m", m=C),
                                    a_hi[:, s % 2, :, :].bitcast(F32), ALU.subtract).then_inc(a_split, 1)

                weight_lo(0)
                weight_lo(1)
                scale_y(it)
                weight_lo(2)
                add_y(it)
                weight_lo(3)
                multiply(0)
                weight_lo(4)
                dve.wait_ge(selT_ready, it + 1)
                V.tensor_copy(gs[0:C, :], ps[0:C, 6, 384:385])
                e = dve.snap((it + 1) & (NE - 1), min_val=0, max_val=NE - 1)
                V.tensor_copy(gcol[:, :].rearrange("p (t e) -> p t e", e=1), gd[:, :, bass.ds(e, 1)])
                for t in range(3):
                    ins = V.tensor_scalar(sel[:, t, :], iota_c[:, :], posr[:, t, bass.ds(it + 1, 1)], None, ALU.is_equal)
                ins.then_inc(sel_ready, 1)
                weight_lo(5)
                multiply(1)
                weight_lo(6)
                act_lo(0)
                for s in range(2, STEPS - 1):
                    weight_lo(3 * s + 1)
                    multiply(s)
                    weight_lo(3 * s + 2)
                    act_lo(s - 1)
                    weight_lo(3 * s + 3)
                weight_lo(UNITS_E - 2)
                multiply(STEPS - 1)
                weight_lo(UNITS_E - 1)
                act_lo(STEPS - 2)
                act_lo(STEPS - 1)
                gather_lo(it + 2)
            scale_y(rounds * NE)
            add_y(rounds * NE)
            dve.wait_ge(scat_added, rounds * (NE * KD) + KD)
            V.sem_inc(resid_done, 1)
            norm(3 * LAYERS, c_fin)
            for t, (t0, rows) in enumerate(TILES):
                for g in range(2):
                    b = take("y")
                    V.tensor_copy(ytok[0:rows, t, 512 * g:512 * g + 512], ps[0:rows, b, :]).then_inc(dve_emptied, 1)
            b = take("small")
            V.tensor_copy(stage3[:, :], ps[0:32, b, 0:P]).then_inc(small_ready, 1)


_INS = ['x_prompt', 'x_sample', 'state_gla', 'state_hgrn', 'state_rglru', 'state_conv', 'cache_mem_k', 'cache_mem_v',
        'mem_prompt', 'norm_mix', 'norm_xattn', 'norm_ffn', 'norm_mem', 'norm_final', 'w_in', 'gla_wa2', 'gla_ba',
        'gla_onorm', 'hg_lb', 'hg_onorm', 'rg_conv_w', 'rg_conv_b', 'rg_wr', 'rg_br', 'rg_wi', 'rg_bi', 'rg_lambda',
        'w_out', 'xa_wq', 'xa_wk', 'xa_wv', 'xa_wo', 'ffd_w1', 'ffd_w3', 'ffd_w2', 'moe_router', 'moe_w1', 'moe_w3',
        'moe_w2']
_OUTS = [(1, 256, 1024), (1, 32, 1024), (2, 1, 4, 48, 96), (2, 1, 4, 64, 96), (2, 1, 256), (2, 1, 3, 256),
         (2, 1, 256, 4, 256), (2, 1, 256, 4, 256), (2, 1, 4, 48, 96), (2, 1, 4, 64, 96), (2, 1, 256), (2, 1, 3, 256)]


def kernel(**inputs):
    import numpy as _np
    import concourse.bacc as _bacc
    from concourse import mybir as _mybir
    from concourse.bass_utils import run_bass_kernel_spmd as _run

    nc = _bacc.Bacc("TRN2", target_bir_lowering=False, num_devices=1)
    arrays, args = {}, []
    for name in _INS:
        a = _np.ascontiguousarray(inputs[name])
        arrays[f"in_{name}_dram"] = a
        args.append(nc.dram_tensor(f"in_{name}_dram", a.shape, _mybir.dt.from_np(a.dtype), kind="ExternalInput").ap())
    for i, shape in enumerate(_OUTS):
        args.append(nc.dram_tensor(f"out_{i}_dram", shape, _mybir.dt.float32, kind="ExternalOutput").ap())
    layer_program(nc, *args)
    r = _run(nc, [arrays], core_ids=[0])
    return tuple(r.results[0][f"out_{i}_dram"] for i in range(len(_OUTS)))
```

```python
from contextlib import ExitStack

import numpy as np

import concourse.bass as bass
from concourse import mybir

F32 = mybir.dt.float32
F32R = mybir.dt.float32r
I32 = mybir.dt.int32
U32 = mybir.dt.uint32
ALU = mybir.AluOpType
ACT = mybir.ActivationFunctionType
AX = mybir.AxisListType

P = 128
D = 1024
KD = D // P
TP, TS = 256, 32
T = TP + TS
TILES = [(0, 128), (128, 128), (256, 32)]
LAYERS = 2
DK_G, DK_H, DV = 48, 64, 96
HEADS = 8
PAIRS = 4
RANK = 16
RG = 256
CONV = 4
MEM = 256
DFF = 2816
FT = DFF // P
STEPS = FT // 2
NE = 8
EPS = 1e-6
CH = 32
NCH = T // CH
LEVELS = [16, 8, 4, 2, 1]
C = 96
MAXR = -(-T // C)

GQ, GK, GV, GR, GA, HQ, HF, HI, HGT, RX, RGT, INW = (
    0, 192, 384, 768, 1152, 1168, 1424, 1680, 2064, 2448, 2704, 2960)

SLOT = 2048
RING = 11
DSLOTS = 3
UNITS_E = 3 * STEPS
SPLITS = 3


def dense_units():
    units = []
    for l in range(LAYERS):
        for key, a, b in (("in", RX, RX + 256), ("in", RGT, RGT + 256), ("in", HF, HF + 256),
                          ("in", GR + 192, GA + RANK), ("in", HQ, HQ + 256),
                          ("in", GV, GV + 192), ("in", GV + 192, GV + 384),
                          ("in", HI, HI + 192), ("in", HI + 192, HI + 384),
                          ("in", GR, GR + 192), ("in", HGT, HGT + 192), ("in", HGT + 192, HGT + 384)):
            units.append((key, l, a, b))
        for key in ("wk", "wv"):
            for j in range(4):
                units.append((key, l, 256 * j, 256 * j + 256))
        for d in range(KD):
            units.append(("out", l, P * d, P * d + P))
        for key in ("wq", "wo"):
            for j in range(4):
                units.append((key, l, 256 * j, 256 * j + 256))
        if l == 0:
            for s in range(STEPS):
                units.append(("w1", l, 256 * s, 256 * s + 256))
                units.append(("w3", l, 256 * s, 256 * s + 256))
            for d in range(KD):
                for half in range(2):
                    units.append(("w2", l, d, half))
    return units


def chunk_plan():
    plan = [("x", "V")] * 6 + [("par", "V")] * 2
    for l in range(LAYERS):
        plan += [("rx", "A")] * 2 + [("rgt", "A")] * 2 + [("q", "A")] * 2 + [("k", "A")] * 2
        plan += [("hf", "A")] * 2 + ([("mem", "A")] * 4 if l == 0 else []) + [("ga", "A")] + [("gate", "A")] * 2 + [("hq", "A")] * 2
        plan += [("v", "A")] * 12 + [("gate", "A")] * 6
        plan += [("kv", "A")] * 5
        plan += [("kdt", "A")] * 3 + [("kv", "A")] * 11
        plan += [("oss", "A")] * 8
        plan += [("out", "V")] * 8
        plan += [("wq", "A")] * 8 + [("kt", "V")] * 8 + [("pt", "A")] * 6 + [("ox", "V")] * 8 + [("wo", "V")] * 8
        if l == 0:
            plan += ([("h1", "A")] * 2 + [("h3", "V")] * 2) * STEPS + [("dn", "V")] * 8
    plan += [("lg", "V")] + [("htok", "A")] * 6 + [("rank", "V")]
    plan += [("y", "V")] * 6 + [("small", "V")]
    return plan


PLAN = chunk_plan()
CHUNK_NO = {}
for _i, (_tag, _e) in enumerate(PLAN):
    CHUNK_NO[_tag, sum(1 for t, _ in PLAN[:_i] if t == _tag)] = _i


def emptied(tag, n):
    i = CHUNK_NO[tag, n]
    return sum(1 for _, e in PLAN[:i + 1] if e == PLAN[i][1])


def layer_program(nc, x_prompt, x_sample, state_gla, state_hgrn, state_rglru, state_conv, cache_mem_k, cache_mem_v,
                  mem_prompt, norm_mix, norm_xattn, norm_ffn, norm_mem, norm_final, w_in, gla_wa2, gla_ba,
                  gla_onorm, hg_lb, hg_onorm, rg_conv_w, rg_conv_b, rg_wr, rg_br, rg_wi, rg_bi, rg_lambda, w_out,
                  xa_wq, xa_wk, xa_wv, xa_wo, ffd_w1, ffd_w3, ffd_w2, moe_router, moe_w1, moe_w3, moe_w2,
                  y_prompt, y_sample, gla_p, hgrn_p, rglru_p, conv_p, mem_k_p, mem_v_p, gla_s, hgrn_s, rglru_s,
                  conv_s):
    units = dense_units()
    at = {}
    with ExitStack() as ctx:
        def sb(name, shape, dt=F32):
            at[name] = (nc.sbuf_base + 31) // 32 * 32
            return ctx.enter_context(nc.sbuf_tensor(name, shape, dt))

        def over(name, shape, offset):
            return nc.alloc_sbuf_tensor_at(name, shape, F32R, offset=offset)

        def sem(name):
            return ctx.enter_context(nc.semaphore(name))

        def view(base, off, *dims):
            n = int(np.prod(dims))
            flat = base[:, off:off + n]
            if len(dims) == 1:
                return flat
            names = " ".join("abcd"[i] for i in range(len(dims)))
            return flat.rearrange(f"p ({names}) -> p {names}", **{"abcd"[i]: dims[i] for i in range(1, len(dims))})

        ring = sb("ring", [P, RING * SLOT])
        xT = sb("xT", [P, KD, T])
        hT = sb("hT", [P, KD, T])
        memT = sb("memT", [P, KD, MEM])
        wqk = sb("wqk", [P, 2, KD, 256])
        kp = sb("kp", [P, 2, D])
        vp = sb("vp", [P, 2, D])
        low = sb("low", [P, 9792])
        s_init = sb("s_init", [P, PAIRS, DV])
        s_fin = sb("s_fin", [P, 2, PAIRS, DV])
        ident = sb("ident", [P, P])
        ones = sb("ones", [P, P])
        iota_e = sb("iota_e", [P, 3, NE])
        restart = sb("restart", [P, T])
        masks = sb("masks", [P, 6, CH], U32)
        par = sb("par", [P, 124])
        par2 = sb("par2", [P, 20])
        wa2 = sb("wa2", [RANK, LAYERS, 256])
        wri = sb("wri", [P, 2, 2, P])
        router = sb("router", [P, KD, NE])
        rstd = sb("rstd", [P, T])
        small = sb("small", [P, 32])
        drv = sb("drv", [P, 64])
        att = sb("att", [P, 2, 16])
        epsc = sb("epsc", [P, 1])
        sq = sb("sq", [P, KD, T])
        more_rounds = sb("more_rounds", [1, 1], I32)
        ps = ctx.enter_context(nc.psum_tensor("ps", [P, 8, 512], F32))

        UP = DSLOTS * SLOT
        q_t = view(ring, UP, PAIRS, T)
        k_t = view(ring, UP + 1152, PAIRS, T)
        b_t = view(ring, UP + 2304, PAIRS, T)
        e_t = view(ring, UP + 3456, PAIRS, T)
        kl_t = view(ring, UP + 4608, PAIRS, T)
        ql_t = view(ring, UP + 5760, PAIRS, T)
        osq = view(ring, UP + 3456, HEADS, T)
        a_full = view(ring, UP + 6912, 3, 4, 2, P)
        s_all = view(ring, UP + 9984, 8, PAIRS, DV)
        memg = view(ring, UP + 13056, KD, MEM)
        xc = view(ring, UP + 15104, 2, CONV - 1 + TP + CONV - 1 + TS)
        u_t = view(ring, UP + 15104 + 588, 2, T)
        ktp = view(ring, UP, KD, MEM)
        kts = view(ring, UP + 2048, KD, MEM)
        qx = view(ring, UP + 4096, KD, T)
        ks = view(ring, UP + 6912, 2, D)
        vs = view(ring, UP + 8960, 2, D)
        pt = view(ring, UP + 11008, 8, T)
        prob = view(ring, UP + 13312, 2, 4, MEM)
        xtok = view(ring, UP, 3, D)
        mtok = view(ring, UP + 6912, 2, D)
        msq = view(ring, UP + 8960, D)
        stage = view(ring, UP + 6144, P)
        stage2 = view(ring, UP + 6272, P)
        prod = view(ring, UP + 12672, 2, T)
        v_tok = view(low, 0, 3, HEADS * DV)
        o_t = view(low, 2304, HEADS, T)
        a_comp = view(low, 2304, 2, 3, 4, CH)
        kd_tok = view(low, 2304 + 768, 3, 512)
        gate = view(low, 4608, HEADS, T)
        la = view(low, 6912, 2, T)
        it_ = view(low, 7488, 2, T)
        tn = view(low, 8064, 2, T)
        gb = view(low, 8640, 2, T)
        gaT = view(low, 9216, T)
        sil0 = view(low, 6912, 2, T)
        htok = view(low, 0, 3, D)
        a_tok = view(low, 4608, 2, 2 * P)
        sil = view(low, 5120, 2, 2 * P)
        y_sb = view(low, 5952, D)
        sel = view(low, 6976, 3, C)
        selT = view(low, 7264, T)
        lgt = view(low, 7936, 3, NE)
        oh1 = view(low, 7960, 3, NE)
        oh2 = view(low, 7984, 3, NE)
        gd = view(low, 8008, 3, NE)
        msel = view(low, 8032, 3, NE)
        tmp8 = view(low, 8056, 3, NE)
        cols = view(low, 8080, 40)
        gcol = view(low, 8120, 3)
        gs = view(low, 8124, 1)
        posr = view(low, 9248, 3, (MAXR + 1) * NE)
        tri = view(low, 9024, P)
        iota_c = view(low, 9152, C)
        ytok = view(low, 0, 3, D)
        stage3 = view(low, 4096, P)
        hg_hi = over("hg_hi", [P, KD, C], at["low"] + 4 * 3072)
        hg_lo = over("hg_lo", [P, KD, C], at["low"] + 4 * 3840)
        a_hi = over("a_hi", [P, 2, 2, C], at["low"] + 4 * 8256)
        a_lo = over("a_lo", [P, 2, 2, C], at["low"] + 4 * 8640)
        h_hi = over("h_hi", [P, KD, T], at["low"])
        h_lo = over("h_lo", [P, KD, T], at["low"] + 4 * 2304)
        ff_hi = over("ff_hi", [P, FT, T], at["ring"] + 4 * UP)
        ff_lo = over("ff_lo", [P, FT, T], at["ring"] + 4 * (UP + FT * T))
        dw_hi = [over("dw_hi0", [P, SLOT], at["low"] + 4 * 4608), over("dw_hi1", [P, SLOT], at["low"] + 4 * 7488)]
        mg_hi = over("mg_hi", [P, KD, MEM], at["low"] + 4 * 7488)
        mg_lo = over("mg_lo", [P, KD, MEM], at["ring"] + 4 * (UP + 13056))
        kvw_hi = [over("kvw_hi0", [P, SLOT], at["sq"]), over("kvw_hi1", [P, SLOT], at["hT"])]
        dw_lo = over("dw_lo", [P, DSLOTS * SLOT], at["ring"])
        w_hi = over("w_hi", [P, SPLITS * SLOT], at["hT"])
        w_lo = over("w_lo", [P, SPLITS * SLOT], at["hT"] + 4 * SPLITS * SLOT)

        c_mix, c_xa, c_ff, c_mem, c_fin = 0, 16, 32, 48, 64
        c_lb, c_cb, c_br, c_bi, c_lam, c_cw, c_h0, c_c0 = 72, 76, 80, 84, 88, 92, 108, 112
        v_kA, v_kB, v_fb, v_sp, v_br, v_bi, v_ms = 0, 4, 8, 12, 16, 20, 24

        unit_in = [sem(f"unit_in{i}") for i in range(DSLOTS)]
        moe_in = [sem(f"moe_in{i}") for i in range(RING)]
        params_in = sem("params_in")
        x_in = sem("x_in")
        mem_in = sem("mem_in")
        zeroed = sem("zeroed")
        const_ok = sem("const_ok")
        wqk_in = sem("wqk_in")
        layer_in = sem("layer_in")
        cache_in = sem("cache_in")
        stored = sem("stored")
        y_stored = sem("y_stored")
        work_zeroed = sem("work_zeroed")
        chunk_ready = sem("chunk_ready")
        act_emptied = sem("act_emptied")
        dve_emptied = sem("dve_emptied")
        act_step = sem("act_step")
        dve_step = sem("dve_step")
        pool_step = sem("pool_step")
        mem_normed = sem("mem_normed")
        drv_ready = sem("drv_ready")
        sp_exp = sem("sp_exp")
        lb_exp = sem("lb_exp")
        resid_done = sem("resid_done")
        squares_ready = sem("squares_ready")
        ssq_ready = sem("ssq_ready")
        rstd_ready = sem("rstd_ready")
        normed = sem("normed")
        memg_ready = sem("memg_ready")
        u_ready = sem("u_ready")
        ri_ready = sem("ri_ready")
        ri_used = sem("ri_used")
        la_ready = sem("la_ready")
        tn_ready = sem("tn_ready")
        beta2_ready = sem("beta2_ready")
        beta_ready = sem("beta_ready")
        hgf_ready = sem("hgf_ready")
        gla_pre = sem("gla_pre")
        gla_ln = sem("gla_ln")
        hg_ln = sem("hg_ln")
        e_ready = sem("e_ready")
        e_exp = sem("e_exp")
        lvl_qk = sem("lvl_qk")
        lvl_ready = sem("lvl_ready")
        lvl_taken = sem("lvl_taken")
        a_ready = sem("a_ready")
        kdec_ready = sem("kdec_ready")
        qdec_ready = sem("qdec_ready")
        kv_ready = sem("kv_ready")
        kv_taken = sem("kv_taken")
        o_ready = sem("o_ready")
        o_taken = sem("o_taken")
        osq_ready = sem("osq_ready")
        ors_ready = sem("ors_ready")
        gate_silu = sem("gate_silu")
        mix_ready = sem("mix_ready")
        sc_ready = sem("sc_ready")
        mx_ready = sem("mx_ready")
        ex_ready = sem("ex_ready")
        pr_ready = sem("pr_ready")
        gap_ready = sem("gap_ready")
        gexp_ready = sem("gexp_ready")
        msel_ready = sem("msel_ready")
        rounds_ready = sem("rounds_ready")
        htok_zero = sem("htok_zero")
        sel_ready = sem("sel_ready")
        gathered = sem("gathered")
        sel_used = sem("sel_used")
        selT_ready = sem("selT_ready")
        ring_free = sem("ring_free")
        dw_hi_done = sem("dw_hi_done")
        dw_split = sem("dw_split")
        h_hi_done = sem("h_hi_done")
        mg_hi_done = sem("mg_hi_done")
        mg_split = sem("mg_split")
        h_split = sem("h_split")
        ff_hi_done = sem("ff_hi_done")
        ff_split = sem("ff_split")
        w2_half = sem("w2_half")
        kv_stored = sem("kv_stored")
        w_used = sem("w_used")
        hi_done = sem("hi_done")
        lo_done = sem("lo_done")
        hg_hi_done = sem("hg_hi_done")
        hg_ready = sem("hg_ready")
        silu_ready = sem("silu_ready")
        act_ready = sem("act_ready")
        a_turned = sem("a_turned")
        a_hi_done = sem("a_hi_done")
        a_split = sem("a_split")
        y_scaled = sem("y_scaled")
        scat_ready = sem("scat_ready")
        scat_added = sem("scat_added")
        small_ready = sem("small_ready")

        block = ctx.enter_context(nc.Block())
        by_feature = "(k p) n -> p k n"

        unit_last = []
        cn = {t: 0 for t, _ in PLAN}

        def last_of(tag, m):
            cn[tag] += m
            return CHUNK_NO[tag, cn[tag] - 1]

        for key, l, a, b in units:
            if key == "in":
                tag, m = {RX: ("rx", 2), RGT: ("rgt", 2), HF: ("hf", 2), HQ: ("hq", 2)}.get(a, (None, 0))
                if a == GR + 192:
                    last_of("ga", 1)
                    tag, m = "gate", 2
                elif tag is None:
                    tag, m = ("v", 3) if GV <= a < GR or HI <= a < HGT else ("gate", 2)
                unit_last.append(last_of(tag, m))
            elif key in ("wk", "wv"):
                unit_last.append(last_of("kv", 2))
            elif key == "out":
                unit_last.append(last_of("out", 1))
            elif key in ("wq", "wo"):
                unit_last.append(last_of(key, 2))
            elif key == "w1":
                unit_last.append(last_of("h1", 2))
            elif key == "w3":
                unit_last.append(last_of("h3", 2))
            else:
                unit_last.append(CHUNK_NO["dn", a])
        landed, total = [], [0] * DSLOTS
        for n, (key, l, a, b) in enumerate(units):
            total[n % DSLOTS] += 32 if key == "out" else 16
            landed.append(total[n % DSLOTS])
        DENSE_LAST = CHUNK_NO["wo", 8 * LAYERS - 1] + 1
        ATT_LAST = CHUNK_NO["ox", 8 * LAYERS - 1] + 1

        SPLIT_UNITS = [n for n, unit in enumerate(units) if unit[0] != "in" and unit[0] != "out"]
        H_BASE = {1: 0, 2: 2 * KD, 4: 3 * KD}
        SPLIT_NORM = {1: 0, 2: KD, 4: 2 * KD}

        def unit_used(eng, n):
            key, l, a, b = units[n]
            if key == "w2" and b == 0:
                eng.wait_ge(w2_half, a + 1)
            else:
                eng.wait_ge(chunk_ready, unit_last[n] + 1)

        def hi_place(n, m):
            return (kvw_hi if units[n][0] in ("wk", "wv") else dw_hi)[m % 2]

        def unit_words(n):
            return STEPS * P if units[n][0] == "w2" else SLOT

        def slot(n, *dims):
            return view(ring, (n % DSLOTS) * SLOT, *dims)

        def unit_of(kind, s):
            if kind == 2:
                return 3 * s + 6 if s < STEPS - 2 else s + 2 * STEPS
            return (2 * s if s < 2 else 3 * s - 2) + kind

        of_unit = {unit_of(kind, s): (kind, s) for s in range(STEPS) for kind in range(3)}

        def moe_slot(u):
            return (u + DSLOTS) % RING

        def as_kind(base, off, kind):
            return view(base, off, 2, D) if kind == 2 else view(base, off, KD, 256)

        @block.sync
        def _(sp):
            sp.dma_start(xtok[:, 0:2, :], x_prompt[0].rearrange("(t p) d -> p t d", p=P)).then_inc(x_in, 16)
            sp.dma_start(xtok[0:TS, 2, :], x_sample[0]).then_inc(x_in, 16)
            sp.wait_ge(params_in, 16 * 17)
            mats = {"in": w_in, "wk": xa_wk, "wv": xa_wv, "wq": xa_wq, "wo": xa_wo, "w1": ffd_w1, "w3": ffd_w3}
            qk_of = {("in", l, HF): l for l in range(LAYERS)}
            for n, (key, l, a, b) in enumerate(units):
                if n == 2:
                    sp.dma_start(mtok[:, :, :], mem_prompt[0].rearrange("(t p) d -> p t d", p=P)).then_inc(mem_in, 16)
                if (key, l, a) in qk_of:
                    if l:
                        sp.wait_ge(chunk_ready, CHUNK_NO["k", 2 * l - 1] + 1)
                    else:
                        sp.wait_ge(zeroed, 2)
                    for i, off in enumerate((GQ, GK)):
                        for h in range(4):
                            sp.dma_start(wqk[:, i, :, 64 * h:64 * h + DK_G],
                                         w_in[l][:, off + DK_G * h:off + DK_G * (h + 1)].rearrange(
                                             by_feature, p=P)).then_inc(wqk_in, 16)
                if n >= DSLOTS:
                    unit_used(sp, n - DSLOTS)
                arrived = unit_in[n % DSLOTS]
                if key == "out":
                    sp.dma_start(slot(n, 10, P)[0:DV, 0:8, :],
                                 w_out[l][0:HEADS * DV, a:b].rearrange("(k p) n -> p k n", p=DV)).then_inc(arrived, 16)
                    sp.dma_start(slot(n, 10, P)[:, 8:10, :],
                                 w_out[l][HEADS * DV:, a:b].rearrange(by_feature, p=P)).then_inc(arrived, 16)
                elif key == "w2":
                    sp.dma_start(slot(n, STEPS, P),
                                 ffd_w2[0][STEPS * P * b:STEPS * P * (b + 1), P * a:P * a + P].rearrange(
                                     by_feature, p=P)).then_inc(arrived, 16)
                else:
                    sp.dma_start(slot(n, KD, b - a),
                                 mats[key][l][:, a:b].rearrange(by_feature, p=P)).then_inc(arrived, 16)
            def load(it, e, u, first=False):
                kind, s = of_unit[u]
                if u >= RING or not first:
                    sp.wait_ge(lo_done, it * UNITS_E + u - RING + 1)
                elif moe_slot(u) < DSLOTS:
                    sp.wait_ge(chunk_ready, DENSE_LAST)
                else:
                    sp.wait_ge(ring_free, 1)
                dst = as_kind(ring, moe_slot(u) * SLOT, kind)
                if kind == 2:
                    src = moe_w2[0, bass.ds(e, 1), 256 * s:256 * s + 256, :].rearrange(
                        "e (k p) n -> p (e k) n", p=P)
                else:
                    w = moe_w3 if kind else moe_w1
                    src = w[0, bass.ds(e, 1), :, 256 * s:256 * s + 256].rearrange("e (k p) n -> p (e k) n", p=P)
                sp.dma_start(dst, src).then_inc(moe_in[moe_slot(u)], 16)

            for u in range(RING):
                load(0, 0, u, True)
            sp.wait_ge(rounds_ready, 1)
            more = sp.value_load(more_rounds[0:1, 0:1], min_val=0, max_val=MAXR - 1)
            for u in range(RING, UNITS_E):
                load(0, 0, u, True)
            with sp.Fori(1, more * NE + NE) as it:
                e = it & (NE - 1)
                sp.lower_val(e)
                for u in range(UNITS_E):
                    load(it, e, u)
            sp.wait_ge(dve_emptied, emptied("y", 5))
            sp.dma_start(y_prompt[0].rearrange("(t p) d -> p t d", p=P), ytok[:, 0:2, :]).then_inc(y_stored, 16)
            sp.dma_start(y_sample[0], ytok[0:TS, 2, :]).then_inc(y_stored, 16)
            sp.wait_ge(y_stored, 32)

        @block.gpsimd
        def _(pool):
            n_step = [0]

            def link(ins):
                n_step[0] += 1
                ins.then_inc(pool_step, 1)
                pool.wait_ge(pool_step, n_step[0])

            link(pool.memset(ones[:, :], 1.0))
            link(pool.memset(ident[:, :], 0.0))
            link(pool.affine_select(out=ident[:, :], in_=ident[:, :], compare_op=ALU.not_equal, fill=1.0, base=0,
                                    pattern=[[-1, P]], channel_multiplier=1))
            pool.sem_inc(const_ok, 1)
            link(pool.memset(restart[:, :], 1.0))
            link(pool.memset(restart[:, :].rearrange("p (c t) -> p c t", t=CH)[:, :, 0:1], 0.0))
            link(pool.iota(iota_e[:, :, :], [[0, 3], [1, NE]], base=-NE, channel_multiplier=0,
                           allow_small_or_imprecise_dtypes=True))
            link(pool.iota(view(low, 0, CH).bitcast(I32), [[0, CH]], base=0, channel_multiplier=1))
            link(pool.iota(view(low, 64, CH).bitcast(I32), [[1, CH]], base=0, channel_multiplier=0))
            link(pool.memset(wa2[:, :, :], 0.0))
            link(pool.memset(wri[:, :, :, :], 0.0))
            link(pool.memset(s_init[:, :, :], 0.0))
            pool.sem_inc(const_ok, 1)
            pool.dma_start(router[:, :, :], moe_router[0].rearrange(by_feature, p=P)).then_inc(layer_in, 16)
            for l in range(LAYERS):
                for h in range(4):
                    pool.dma_start(wa2[:, l, 64 * h:64 * h + DK_G],
                                   gla_wa2[l][:, DK_G * h:DK_G * (h + 1)]).then_inc(layer_in, 16)
            for l in range(LAYERS):
                if l:
                    pool.wait_ge(ri_ready, l)
                    pool.wait_ge(o_ready, 8 * l)
                    pool.wait_ge(kv_taken, 9 * l)
                    pool.wait_ge(chunk_ready, CHUNK_NO["wo", 8 * l - 1] + 1)
                for i, w in enumerate((rg_wr, rg_wi)):
                    for blk in range(4):
                        r0 = 64 * (blk % 2)
                        pool.dma_start(wri[r0:r0 + 64, i, blk // 2, r0:r0 + 64], w[l, blk]).then_inc(layer_in, 16)
                for h in range(4):
                    r0 = 64 * (h % 2)
                    pool.dma_start(s_init[r0:r0 + DK_G, h // 2, :], state_gla[l, 0, h]).then_inc(layer_in, 16)
                    pool.dma_start(s_init[r0:r0 + DK_H, 2 + h // 2, :], state_hgrn[l, 0, h]).then_inc(layer_in, 16)
                pool.wait_ge(chunk_ready, CHUNK_NO[("dn", 7) if l else ("mem", 3)] + 1)
                link(pool.memset(a_full[:, :, :, :, :], 0.0))
                link(pool.memset(s_all[:, 0, :, :], 0.0))
                pool.sem_inc(work_zeroed, 1)
                pool.wait_ge(act_emptied, emptied("kv", 16 * l + 15))
                pool.dma_start(mem_k_p[l, 0].rearrange("(t p) h d -> p t (h d)", p=P), kp[:, :, :]).then_inc(kv_stored, 16)
                pool.dma_start(mem_v_p[l, 0].rearrange("(t p) h d -> p t (h d)", p=P), vp[:, :, :]).then_inc(kv_stored, 16)
                pool.wait_ge(o_ready, 8 * (l + 1))
                pool.dma_start(ks[:, :, :], cache_mem_k[l, 0].rearrange("(t p) h d -> p t (h d)", p=P)).then_inc(cache_in, 16)
                pool.dma_start(vs[:, :, :], cache_mem_v[l, 0].rearrange("(t p) h d -> p t (h d)", p=P)).then_inc(cache_in, 16)
                pool.wait_ge(kv_taken, 9 * (l + 1))
                for g, (go, ho) in enumerate(((gla_p, hgrn_p), (gla_s, hgrn_s))):
                    for h in range(4):
                        r0 = 64 * (h % 2)
                        pool.dma_start(go[l, 0, h], s_fin[r0:r0 + DK_G, g, h // 2, :]).then_inc(stored, 16)
                        pool.dma_start(ho[l, 0, h], s_fin[r0:r0 + DK_H, g, 2 + h // 2, :]).then_inc(stored, 16)
            pool.wait_ge(chunk_ready, DENSE_LAST)
            link(pool.affine_select(out=tri[:, :], in_=ones[:, :], compare_op=ALU.is_gt, fill=0.0, base=0,
                                    pattern=[[1, P]], channel_multiplier=-1))
            link(pool.iota(iota_c[:, :], [[1, C]], base=0, channel_multiplier=0, allow_small_or_imprecise_dtypes=True))
            pool.sem_inc(const_ok, 1)
            pool.wait_ge(small_ready, 1)
            for (dst, a, n, pat) in ((rglru_p, 0, 4, "l b (k p) -> (l b k) p"), (rglru_s, 4, 4, "l b (k p) -> (l b k) p"),
                                     (conv_p, 8, 12, "l b j (k p) -> (l b j k) p"),
                                     (conv_s, 20, 12, "l b j (k p) -> (l b j k) p")):
                pool.dma_start(dst.rearrange(pat, p=P), stage3[a:a + n, :]).then_inc(stored, 16)
            pool.wait_ge(stored, 16 * (16 * LAYERS + 4))
            pool.wait_ge(kv_stored, 16 * 2 * LAYERS)

        @block.tensor
        def _(pe):
            state = {"c": 0, "u": 0, "m": 0}

            def mm(out, lhsT, rhs, first, last):
                return nc.tensor.matmul(out, lhsT, rhs, start=first, stop=last)

            def open_bank(tag):
                c = state["c"]
                assert PLAN[c][0] == tag, (c, PLAN[c], tag)
                if c >= 4:
                    who = PLAN[c - 4][1]
                    n = sum(1 for _, e in PLAN[:c - 3] if e == who)
                    pe.wait_ge(act_emptied if who == "A" else dve_emptied, n)
                return c % 4

            def close_bank(ins):
                ins.then_inc(chunk_ready, 1)
                state["c"] += 1

            def next_unit(*dims):
                n = state["u"]
                state["u"] += 1
                pe.wait_ge(unit_in[n % DSLOTS], landed[n])
                return slot(n, *dims)

            def project(tag, w, m0, m, rhs, n, fresh=None):
                b = open_bank(tag)
                for k in range(KD):
                    if fresh is not None:
                        pe.wait_ge(normed, KD * fresh + k + 1)
                    last = mm(ps[0:m, b, 0:n], w[:, k, m0:m0 + m], rhs[:, k, 0:n], k == 0, k == KD - 1)
                close_bank(last)

            def next_split_unit(*dims):
                n, m = state["u"], state["m"]
                assert SPLIT_UNITS[m] == n
                state["u"] += 1
                state["m"] += 1
                pe.wait_ge(dw_split, m + 1)
                return view(hi_place(n, m), 0, *dims), view(dw_lo, (n % DSLOTS) * SLOT, *dims)

            def split_mm(out, xh, xl, wh, wl, first, last):
                mm(out, xh, wh, first, False)
                mm(out, xh, wl, False, False)
                return mm(out, xl, wh, False, last)

            def project_split(tag, w, m0, wait_tile=None):
                b = open_bank(tag)
                for k in range(KD):
                    if wait_tile is not None:
                        wait_tile(k)
                    last = split_mm(ps[:, b, 0:T], w[0][:, k, m0:m0 + P], w[1][:, k, m0:m0 + P],
                                    h_hi[:, k, :], h_lo[:, k, :], k == 0, k == KD - 1)
                close_bank(last)

            def norm_tile(i):
                return lambda k: pe.wait_ge(h_split, SPLIT_NORM[i] + k + 1)

            def project_tokens(tag, w, width, act, t0, rows):
                b = open_bank(tag)
                for k in range(KD):
                    last = mm(ps[0:rows, b, 0:width], act[:, k, t0:t0 + rows], w[:, k, 0:width], k == 0, k == KD - 1)
                close_bank(last)

            def sum_squares(i):
                for k in range(KD):
                    pe.wait_ge(squares_ready, KD * i + k + 1)
                    last = mm(ps[:, 7, 0:T], ones[:, :], sq[:, k, :], k == 0, k == KD - 1)
                last.then_inc(ssq_ready, 1)

            pe.wait_ge(const_ok, 1)
            pe.wait_ge(x_in, 32)
            for t, (t0, rows) in enumerate(TILES):
                for g in range(2):
                    b = open_bank("x")
                    for j in range(4):
                        d = 4 * g + j
                        last = nc.tensor.transpose(ps[:, b, P * j:P * j + rows], xtok[0:rows, t, P * d:P * d + P],
                                                   ident[0:rows, 0:rows])
                    close_bank(last)
            pe.wait_ge(params_in, 16 * 17)
            b = open_bank("par")
            close_bank(nc.tensor.transpose(ps[:, b, 0:124], stage[0:124, :], ident[0:124, 0:124]))
            b = open_bank("par")
            close_bank(nc.tensor.transpose(ps[:, b, 0:20], stage2[0:20, :], ident[0:20, 0:20]))

            def level(l, idx):
                if idx >= 2:
                    pe.wait_ge(lvl_taken, 6 * l + idx - 1)
                if idx:
                    pe.wait_ge(lvl_qk, 5 * l + idx)
                kk, qq = (kl_t, ql_t) if idx else (k_t, q_t)
                b0 = 4 if idx % 2 else 6
                for c in range(NCH):
                    t0, tile, r0 = CH * c, c // 4, CH * (c % 4)
                    for h in range(HEADS):
                        p0, pr = 64 * (h % 2), h // 2
                        col = (tile * 4 + pr) * CH
                        last = mm(ps[r0:r0 + CH, b0 + h % 2, col:col + CH], kk[p0:p0 + 64, pr, t0:t0 + CH],
                                  qq[p0:p0 + 64, pr, t0:t0 + CH], True, True)
                last.then_inc(lvl_ready, 1)

            def kv_unit(j0, n):
                for j in range(j0, j0 + n):
                    if j % 2 == 0:
                        state["kvw"] = next_split_unit(KD, 256)
                    wh, wl = state["kvw"]
                    t0 = P * (j % 2)
                    b_ = open_bank("kv")
                    for k in range(KD):
                        last_ = split_mm(ps[:, b_, 0:256], mg_hi[:, k, t0:t0 + P], mg_lo[:, k, t0:t0 + P],
                                         wh[:, k, :], wl[:, k, :], k == 0, k == KD - 1)
                    close_bank(last_)

            for l in range(LAYERS):
                sum_squares(3 * l)
                w = next_unit(KD, 256)
                for j in range(2):
                    project("rx", w, P * j, P, hT, T, 3 * l if j == 0 else None)
                w = next_unit(KD, 256)
                for j in range(2):
                    project("rgt", w, P * j, P, hT, T)
                pe.wait_ge(wqk_in, 128 * (l + 1))
                for i, tag in enumerate("qk"):
                    for j in range(2):
                        project(tag, wqk[:, i], P * j, P, hT, T)
                w = next_unit(KD, 256)
                for j in range(2):
                    project("hf", w, P * j, P, hT, T)
                if l == 0:
                    pe.wait_ge(mem_normed, 1)
                    for t in range(2):
                        for g in range(2):
                            b = open_bank("mem")
                            for j in range(4):
                                d = 4 * g + j
                                last = nc.tensor.transpose(ps[:, b, P * j:P * j + P], mtok[:, t, P * d:P * d + P], ident[:, :])
                            close_bank(last)
                pe.wait_ge(u_ready, l + 1)
                pe.wait_ge(layer_in, 16 * (9 + 16 * (l + 1)))
                for i in range(2):
                    for j in range(2):
                        last = mm(ps[:, 4 + 2 * i + j, 0:T], wri[:, i, j, :], u_t[:, j, :], True, True)
                last.then_inc(ri_ready, 1)
                w = next_unit(KD, 208)
                project("ga", w, 192, RANK, hT, T)
                for j in range(2):
                    project("gate", w, DV * j, DV, hT, T)
                w = next_unit(KD, 256)
                for j in range(2):
                    project("hq", w, P * j, P, hT, T)

                def values():
                    w_ = next_unit(KD, 192)
                    for t0, rows in TILES:
                        project_tokens("v", w_, 192, hT, t0, rows)

                def gates():
                    w_ = next_unit(KD, 192)
                    for j in range(2):
                        project("gate", w_, DV * j, DV, hT, T)

                pe.wait_ge(ri_used, l + 1)
                pe.wait_ge(act_emptied, emptied("ga", l))
                for j in range(2):
                    last = mm(ps[:, 4 + j, 0:T], wa2[:, l, P * j:P * j + P], gaT[0:RANK, :], True, True)
                last.then_inc(gla_pre, 1)
                values()
                pe.wait_ge(act_emptied, emptied("hq", 2 * l + 1))
                pe.wait_ge(hgf_ready, l + 1)
                level(l, 0)
                values()
                values()
                level(l, 1)
                values()
                level(l, 2)
                gates()
                level(l, 3)
                gates()
                level(l, 4)
                gates()
                level(l, 5)
                pe.wait_ge(mg_split, l + 1)
                if l:
                    pe.wait_ge(stored, 16 * 16 * l)
                    pe.wait_ge(kv_stored, 16 * 2 * l)
                kv_unit(0, 5)
                pe.wait_ge(kdec_ready, l + 1)
                for t, (t0, rows) in enumerate(TILES):
                    b = open_bank("kdt")
                    for pr in range(PAIRS):
                        last = nc.tensor.transpose(ps[0:rows, b, P * pr:P * pr + P], kl_t[:, pr, t0:t0 + rows],
                                                   ident[:, :])
                    close_bank(last)
                kv_unit(5, 1)
                pe.wait_ge(act_emptied, emptied("kdt", 3 * l + 2))
                pe.wait_ge(lvl_taken, 6 * (l + 1))
                for c in range(NCH):
                    tile, r0 = c // 4, CH * (c % 4)
                    if c >= 4:
                        pe.wait_ge(kv_taken, 9 * l + c - 3)
                    for h in range(HEADS):
                        p0, pr = 64 * (h % 2), h // 2
                        last = mm(ps[p0:p0 + 64, 4 + c % 4, DV * pr:DV * pr + DV],
                                  kd_tok[r0:r0 + CH, tile, P * pr + p0:P * pr + p0 + 64],
                                  v_tok[r0:r0 + CH, tile, DV * h:DV * h + DV], True, True)
                    last.then_inc(kv_ready, 1)
                    if c in (4, 6):
                        kv_unit(6 + (c - 4), 2)
                kv_unit(10, 6)
                pe.wait_ge(kv_taken, 9 * (l + 1))
                pe.wait_ge(a_ready, l + 1)
                pe.wait_ge(qdec_ready, l + 1)
                for g in range(2):
                    if g:
                        pe.wait_ge(o_taken, 8 * l + 4)
                    for h in range(4 * g, 4 * g + 4):
                        for t, (t0, rows) in enumerate(TILES):
                            mm(ps[0:DV, 4 + h % 4, t0:t0 + rows], v_tok[0:rows, t, DV * h:DV * h + DV],
                               a_full[0:rows, t, h // 2, h % 2, 0:rows], t == 0, False)
                    for c in range(NCH):
                        for h in range(4 * g, 4 * g + 4):
                            p0, pr = 64 * (h % 2), h // 2
                            s = s_all[p0:p0 + 64, c, pr, :] if c < 8 else s_init[p0:p0 + 64, pr, :]
                            last = mm(ps[0:DV, 4 + h % 4, CH * c:CH * c + CH], s, ql_t[p0:p0 + 64, pr, CH * c:CH * c + CH],
                                      False, c == NCH - 1)
                            if c == NCH - 1:
                                last.then_inc(o_ready, 1)
                for h in range(HEADS):
                    pe.wait_ge(osq_ready, 8 * l + h + 1)
                    b = open_bank("oss")
                    close_bank(mm(ps[0:DV, b, 0:T], ones[0:DV, 0:DV], osq[0:DV, h, :], True, True))
                for d in range(KD):
                    w = next_unit(10, P)
                    b = open_bank("out")
                    for h in range(HEADS):
                        if d == 0:
                            pe.wait_ge(mix_ready, HEADS * l + h + 1)
                        mm(ps[:, b, 0:T], w[0:DV, h, :], o_t[0:DV, h, :], h == 0, False)
                    for j in range(2):
                        last = mm(ps[:, b, 0:T], w[:, 8 + j, :], la[:, j, :], False, j == 1)
                    close_bank(last)
                sum_squares(3 * l + 1)
                for i in range(4):
                    w = next_split_unit(KD, 256)
                    for j in range(2):
                        project_split("wq", w, P * j, norm_tile(3 * l + 1) if i == j == 0 else None)
                for g in range(2):
                    if g:
                        pe.wait_ge(cache_in, 32 * (l + 1))
                    for t in range(2):
                        for q4 in range(2):
                            b = open_bank("kt")
                            for j in range(4):
                                d = 4 * q4 + j
                                last = nc.tensor.transpose(ps[:, b, P * j:P * j + P],
                                                           (ks if g else kp)[:, t, P * d:P * d + P], ident[:, :])
                            close_bank(last)
                pe.wait_ge(act_emptied, emptied("wq", 8 * l + 7))
                pe.wait_ge(dve_emptied, emptied("kt", 8 * l + 7))

                def scores(t):
                    t0, rows = TILES[t]
                    if t == 2:
                        pe.wait_ge(ex_ready, 3 * l + 1)
                    keys = kts if t == 2 else ktp
                    for h in range(4):
                        bank = (6 if t == 1 else 4) + h // 2
                        for j in range(2):
                            last = mm(ps[0:rows, bank, MEM * (h % 2):MEM * (h % 2) + MEM], qx[:, 2 * h + j, t0:t0 + rows],
                                      keys[:, 2 * h + j, :], j == 0, j == 1)
                    last.then_inc(sc_ready, 1)

                def turn_probs(t):
                    t0, rows = TILES[t]
                    pe.wait_ge(pr_ready, 3 * l + t + 1)
                    for g in range(2):
                        b = open_bank("pt")
                        for j in range(4):
                            h, m = 2 * g + j // 2, j % 2
                            last = nc.tensor.transpose(ps[:, b, P * j:P * j + rows],
                                                       prob[0:rows, t % 2, h, P * m:P * m + P], ident[0:rows, 0:rows])
                        close_bank(last)

                scores(0)
                scores(1)
                turn_probs(0)
                scores(2)
                turn_probs(1)
                turn_probs(2)
                pe.wait_ge(act_emptied, emptied("pt", 6 * l + 5))
                for d in range(KD):
                    b = open_bank("ox")
                    h = d // 2
                    for m in range(2):
                        mm(ps[:, b, 0:TP], vp[:, m, P * d:P * d + P], pt[:, 2 * h + m, 0:TP], m == 0, m == 1)
                    for m in range(2):
                        last = mm(ps[:, b, TP:T], vs[:, m, P * d:P * d + P], pt[:, 2 * h + m, TP:T], m == 0, m == 1)
                    close_bank(last)
                for i in range(4):
                    w = next_split_unit(KD, 256)
                    for j in range(2):
                        project_split("wo", w, P * j, (lambda k: pe.wait_ge(dve_emptied, emptied("ox", 8 * l + k)))
                                      if i == j == 0 else None)
                    if l == LAYERS - 1 and i == 0:
                        pe.wait_ge(chunk_ready, ATT_LAST)
                        pe.sem_inc(ring_free, 1)
                sum_squares(3 * l + 2)
                if l == 0:
                    for s in range(STEPS):
                        w = next_split_unit(KD, 256)
                        for j in range(2):
                            project_split("h1", w, P * j, norm_tile(2) if s == j == 0 else None)
                        w = next_split_unit(KD, 256)
                        for j in range(2):
                            project_split("h3", w, P * j)
                    for d in range(KD):
                        b = open_bank("dn")
                        for half in range(2):
                            wh, wl = next_split_unit(STEPS, P)
                            for f in range(STEPS):
                                g = STEPS * half + f
                                if d == 0:
                                    pe.wait_ge(ff_split, g + 1)
                                last = split_mm(ps[:, b, 0:T], wh[:, f, :], wl[:, f, :], ff_hi[:, g, :], ff_lo[:, g, :],
                                                g == 0, g == FT - 1)
                            if half == 0:
                                last.then_inc(w2_half, 1)
                        close_bank(last)

            b = open_bank("lg")
            for t, (t0, rows) in enumerate(TILES):
                for k in range(KD):
                    if t == 0:
                        pe.wait_ge(normed, KD * (3 * LAYERS - 1) + k + 1)
                    last = mm(ps[0:rows, b, NE * t:NE * t + NE], hT[:, k, t0:t0 + rows], router[:, k, :], k == 0, k == KD - 1)
            close_bank(last)
            for t, (t0, rows) in enumerate(TILES):
                for g in range(2):
                    b = open_bank("htok")
                    for j in range(4):
                        last = nc.tensor.transpose(ps[0:rows, b, P * j:P * j + P], hT[:, 4 * g + j, t0:t0 + rows],
                                                   ident[:, :])
                    close_bank(last)
            pe.wait_ge(chunk_ready, CHUNK_NO["htok", 5] + 1)
            pe.sem_inc(w_used, SPLITS)
            pe.wait_ge(msel_ready, 1)
            pe.wait_ge(const_ok, 3)
            b = open_bank("rank")
            for t in range(3):
                for t2 in range(t + 1):
                    mm(ps[:, b, NE * t:NE * t + NE], tri[:, :] if t2 == t else ones[:, :], msel[:, t2, :], t2 == 0, t2 == t)
            for t2 in range(3):
                last = mm(ps[:, b, 3 * NE:4 * NE], ones[:, :], msel[:, t2, :], t2 == 0, t2 == 2)
            close_bank(last)
            pe.wait_ge(rounds_ready, 1)
            pe.wait_ge(act_emptied, emptied("htok", 5))
            more = pe.value_load(more_rounds[0:1, 0:1], min_val=0, max_val=MAXR - 1)

            def gather(n):
                pe.wait_ge(sel_ready, n)
                for d in range(KD):
                    out = ps[:, 5, C * d:C * d + C] if d < 5 else ps[:, 7, C * (d - 5):C * (d - 5) + C]
                    for t in range(3):
                        last = mm(out, htok[:, t, P * d:P * d + P], sel[:, t, :], t == 0, t == 2)
                last.then_inc(gathered, 1)

            def scatter(n):
                pe.wait_ge(y_scaled, n + 1)
                for d in range(KD):
                    if d >= 4:
                        pe.wait_ge(scat_added, n * KD + d - 3)
                    mm(ps[:, 4 + d % 4, 0:T], y_sb[0:C, P * d:P * d + P], selT[0:C, :], True, True).then_inc(scat_ready, 1)

            gather(1)

            def expert(it, last_one):
                def parts(kind, s):
                    u = unit_of(kind, s)
                    pe.wait_ge(lo_done, it * UNITS_E + u + 1)
                    off = (u % SPLITS) * SLOT
                    return as_kind(w_hi, off, kind), as_kind(w_lo, off, kind)

                def up(s):
                    for kind in range(2):
                        wh, wl = parts(kind, s)
                        for k in range(KD):
                            last_ = split_mm(ps[0:C, s % 2, 256 * kind:256 * kind + 256], hg_hi[:, k, :], hg_lo[:, k, :],
                                             wh[:, k, :], wl[:, k, :], k == 0, k == KD - 1)
                        last_.then_inc(w_used, 1)

                def turn(s):
                    pe.wait_ge(act_ready, it * STEPS + s + 1)
                    if s:
                        pe.wait_ge(a_split, it * STEPS + s)
                    for j in range(2):
                        last_ = nc.tensor.transpose(ps[:, 4, C * j:C * j + C], a_tok[0:C, s % 2, P * j:P * j + P],
                                                    ident[0:C, 0:C])
                    last_.then_inc(a_turned, 1)

                def down(s):
                    pe.wait_ge(a_split, it * STEPS + s + 1)
                    wh, wl = parts(2, s)
                    for j in range(2):
                        for half in range(2):
                            cols_ = slice(512 * half, 512 * half + 512)
                            last_ = split_mm(ps[0:C, 2 + half, :], a_hi[:, s % 2, j, :], a_lo[:, s % 2, j, :],
                                             wh[:, j, cols_], wl[:, j, cols_], s == 0 and j == 0,
                                             s == STEPS - 1 and j == 1)
                    last_.then_inc(w_used, 1)

                pe.wait_ge(hg_ready, it + 1)
                up(0)
                scatter(it)
                up(1)
                pe.wait_ge(scat_added, it * KD + KD)
                for t in range(3):
                    nc.tensor.transpose(ps[0:C, 6, P * t:P * t + P], sel[:, t, :], ident[:, :])
                for t in range(3):
                    last = mm(ps[0:C, 6, 384:385], sel[:, t, :], gcol[:, t:t + 1], t == 0, t == 2)
                last.then_inc(sel_used, 1)
                turn(0)
                for s in range(2, STEPS):
                    up(s)
                    turn(s - 1)
                    down(s - 2)
                turn(STEPS - 1)
                if not last_one:
                    gather(it + 2)
                down(STEPS - 2)
                down(STEPS - 1)

            with pe.Fori(0, more * NE + (NE - 1)) as it:
                expert(it, False)
            expert(more * NE + (NE - 1), True)
            scatter(more * NE + NE)

            pe.wait_ge(scat_added, more * (NE * KD) + (NE + 1) * KD)
            sum_squares(3 * LAYERS)
            for t, (t0, rows) in enumerate(TILES):
                for g in range(2):
                    b = open_bank("y")
                    for j in range(4):
                        if t == 0:
                            pe.wait_ge(normed, KD * (3 * LAYERS) + 4 * g + j + 1)
                        last = nc.tensor.transpose(ps[0:rows, b, P * j:P * j + P], hT[:, 4 * g + j, t0:t0 + rows],
                                                   ident[:, :])
                    close_bank(last)
            b = open_bank("small")
            close_bank(nc.tensor.transpose(ps[0:32, b, 0:P], small[:, :], ident[:, :]))

        @block.scalar
        def _(act):
            st = {"c": 0, "n": 0, "s": 0, "m": 0}

            def link(ins):
                st["s"] += 1
                ins.then_inc(act_step, 1)
                act.wait_ge(act_step, st["s"])

            def take(tag):
                while PLAN[st["c"]][1] != "A":
                    st["c"] += 1
                assert PLAN[st["c"]][0] == tag, (PLAN[st["c"]], tag)
                c = st["c"]
                act.wait_ge(chunk_ready, c + 1)
                st["c"] += 1
                return c % 4

            def f(out, in_, func, **kw):
                return nc.scalar.activation(out, in_, func, **kw)

            def unit_hi(count=1):
                for _ in range(count):
                    m = st["m"]
                    n = SPLIT_UNITS[m]
                    st["m"] += 1
                    act.wait_ge(unit_in[n % DSLOTS], landed[n])
                    if m >= 2:
                        unit_used(act, SPLIT_UNITS[m - 2])
                    f(view(hi_place(n, m), 0, unit_words(n)), slot(n, unit_words(n)), ACT.Copy).then_inc(dw_hi_done, 1)

            def norm(i, wait_tile, before={}):
                for d in range(KD):
                    unit_hi(before.get(d, 0))
                    wait_tile(d)
                    f(sq[:, d, :], xT[:, d, :], ACT.Square).then_inc(squares_ready, 1)
                unit_hi(before.get(KD, 0))
                act.wait_ge(ssq_ready, i + 1)
                link(f(rstd[:, :], ps[:, 7, 0:T], ACT.Ln, scale=1.0 / D, bias=epsc[:, 0:1]))
                f(rstd[:, :], rstd[:, :], ACT.Exp, scale=-0.5).then_inc(rstd_ready, 1)
                if i in SPLIT_NORM:
                    for k in range(KD):
                        act.wait_ge(normed, KD * i + k + 1)
                        f(h_hi[:, k, :], hT[:, k, :], ACT.Copy).then_inc(h_hi_done, 1)

            def added(tag, n0):
                return lambda d: act.wait_ge(dve_emptied, emptied(tag, n0 + d))

            act.wait_ge(zeroed, 1)
            row = 0
            for src, n in ((norm_mix, 16), (norm_xattn, 16), (norm_ffn, 16), (norm_mem, 16)):
                act.dma_start(stage[row:row + n, :], src.rearrange("l (k p) -> (l k) p", p=P)).then_inc(params_in, 16)
                row += n
            act.dma_start(stage[row:row + 8, :], norm_final.rearrange("(k p) -> k p", p=P)).then_inc(params_in, 16)
            row += 8
            for src in (hg_lb, rg_conv_b, rg_br, rg_bi, rg_lambda):
                act.dma_start(stage[row:row + 4, :], src.rearrange("l (k p) -> (l k) p", p=P)).then_inc(params_in, 16)
                row += 4
            act.dma_start(stage[row:row + 16, :],
                           rg_conv_w.rearrange("l j (k p) -> (l j k) p", p=P)).then_inc(params_in, 16)
            row += 16
            act.dma_start(stage[row:row + 4, :],
                           state_rglru.rearrange("l b (k p) -> (l b k) p", p=P)).then_inc(params_in, 16)
            row += 4
            act.dma_start(stage[row:row + 12, :],
                           state_conv.rearrange("l b j (k p) -> (l b j k) p", p=P)).then_inc(params_in, 16)
            act.dma_start(stage2[0:8, 0:DV], gla_onorm.rearrange("l (h v) -> (l h) v", v=DV)).then_inc(params_in, 16)
            act.dma_start(stage2[8:16, 0:DV], hg_onorm.rearrange("l (h v) -> (l h) v", v=DV)).then_inc(params_in, 16)
            for par_ in range(2):
                act.dma_start(stage2[16:20, 64 * par_:64 * par_ + DK_G],
                               gla_ba.rearrange("l (g two k) -> (l g) two k", two=2, k=DK_G)[:, par_, :]
                               ).then_inc(params_in, 16)
            for l in range(LAYERS):
                norm(3 * l, added("dn", 0) if l else lambda d: act.wait_ge(resid_done, 1),
                     {d: 2 for d in range(KD - 1)} if l else {})
                if l == 0:
                    act.wait_ge(drv_ready, 2)
                    f(drv[:, 32:36], drv[:, 32:36], ACT.Exp).then_inc(lb_exp, 1)
                    f(drv[:, 36:40], drv[:, 36:40], ACT.Exp, scale=-1.0).then_inc(sp_exp, 1)
                for j in range(2):
                    b = take("rx")
                    if l:
                        act.wait_ge(qdec_ready, l)
                    f(xc[:, j, 3:3 + TP], ps[:, b, 0:TP], ACT.Copy)
                    f(xc[:, j, 6 + TP:6 + TP + TS], ps[:, b, TP:T], ACT.Copy).then_inc(act_emptied, 1)
                for j in range(2):
                    b = take("rgt")
                    f(gb[:, j, :], ps[:, b, 0:T], ACT.Gelu_apprx_tanh).then_inc(act_emptied, 1)
                for j in range(2):
                    b = take("q")
                    f(q_t[:, j, :], ps[:, b, 0:T], ACT.Copy, scale=float(DK_G) ** -0.5).then_inc(act_emptied, 1)
                for j in range(2):
                    b = take("k")
                    f(k_t[:, j, :], ps[:, b, 0:T], ACT.Copy).then_inc(act_emptied, 1)
                if l == 0:
                    act.wait_ge(mem_in, 16)
                    act.wait_ge(drv_ready, 1)
                    for t in range(2):
                        link(f(msq[:, :], mtok[:, t, :], ACT.Square, accum_out=drv[:, v_ms + t:v_ms + t + 1]))
                    link(f(drv[:, v_ms:v_ms + 2], drv[:, v_ms:v_ms + 2], ACT.Ln, scale=1.0 / D, bias=epsc[:, 0:1]))
                    link(f(drv[:, v_ms:v_ms + 2], drv[:, v_ms:v_ms + 2], ACT.Exp, scale=-0.5))
                    for t in range(2):
                        link(f(mtok[:, t, :], mtok[:, t, :], ACT.Copy, scale=drv[:, v_ms + t:v_ms + t + 1]))
                    act.sem_inc(mem_normed, 1)
                for j in range(2):
                    b = take("hf")
                    f(e_t[:, 2 + j, :], ps[:, b, 0:T], ACT.Tanh, scale=0.5).then_inc(act_emptied, 1)
                if l == 0:
                    for t in range(2):
                        for g in range(2):
                            b = take("mem")
                            f(memT[:, 4 * g:4 * g + 4, P * t:P * t + P],
                              ps[:, b, :].rearrange("p (j m) -> p j m", m=P), ACT.Copy).then_inc(act_emptied, 1)
                act.wait_ge(ri_ready, l + 1)
                for i, dst in enumerate((la, it_)):
                    for j in range(2):
                        ins = f(dst[:, j, :], ps[:, 4 + 2 * i + j, 0:T], ACT.Tanh, scale=0.5,
                                bias=drv[:, (v_br, v_bi)[i] + 2 * l + j:(v_br, v_bi)[i] + 2 * l + j + 1])
                ins.then_inc(ri_used, 1)
                b = take("ga")
                f(gaT[0:RANK, :], ps[0:RANK, b, 0:T], ACT.Copy).then_inc(act_emptied, 1)

                def gate_copy(h):
                    b_ = take("gate")
                    f(gate[0:DV, h, :], ps[0:DV, b_, 0:T], ACT.Copy).then_inc(act_emptied, 1)

                gate_copy(2)
                gate_copy(3)
                for j in range(2):
                    b = take("hq")
                    f(q_t[:, 2 + j, :], ps[:, b, 0:T], ACT.Silu).then_inc(act_emptied, 1)
                act.wait_ge(la_ready, l + 1)
                f(tn[:, :, :], la[:, :, :], ACT.Tanh, scale=-1.0).then_inc(tn_ready, 1)

                def value_copy(n):
                    for t, (t0, rows) in enumerate(TILES):
                        b_ = take("v")
                        f(v_tok[0:rows, t, 192 * n:192 * n + 192], ps[0:rows, b_, 0:192], ACT.Copy).then_inc(act_emptied, 1)

                def kv_copy(j0, n):
                    for j in range(j0, j0 + n):
                        b_ = take("kv")
                        dst = kp if j < 8 else vp
                        o = 256 * (j % 8 // 2)
                        f(dst[:, j % 2, o:o + 256], ps[:, b_, 0:256], ACT.Copy).then_inc(act_emptied, 1)
                        if j % 2 and j < 12:
                            unit_hi()

                value_copy(0)
                act.wait_ge(gla_pre, l + 1)
                act.wait_ge(hgf_ready, l + 1)
                for j in range(2):
                    ins = f(e_t[:, j, :], ps[:, 4 + j, 0:T], ACT.Abs, bias=par2[:, 16 + 2 * l + j:17 + 2 * l + j])
                link(ins)
                link(f(e_t[:, 0:2, :], e_t[:, 0:2, :], ACT.Exp, scale=-1.0))
                f(e_t[:, 0:2, :], e_t[:, 0:2, :], ACT.Ln, bias=1.0).then_inc(gla_ln, 1)
                f(kl_t[:, 2:4, :], ql_t[:, 2:4, :], ACT.Ln).then_inc(hg_ln, 1)
                act.wait_ge(tn_ready, l + 1)
                f(la[:, :, :], la[:, :, :], ACT.Exp).then_inc(beta_ready, 1)
                def level_exp(i):
                    act.wait_ge(e_ready, 6 * l + i + 1)
                    f(e_t[:, :, :], e_t[:, :, :], ACT.Exp).then_inc(e_exp, 1)

                value_copy(1)
                level_exp(0)
                act.wait_ge(beta2_ready, l + 1)
                link(f(tn[:, :, :], tn[:, :, :], ACT.Ln))
                f(tn[:, :, :], tn[:, :, :], ACT.Exp, scale=0.5).then_inc(beta_ready, 1)
                value_copy(2)
                level_exp(1)
                value_copy(3)
                level_exp(2)
                gate_copy(0)
                gate_copy(1)
                level_exp(3)
                gate_copy(4)
                gate_copy(5)
                level_exp(4)
                act.wait_ge(memg_ready, l + 1)
                f(mg_hi[:, :, :], memg[:, :, :], ACT.Copy).then_inc(mg_hi_done, 1)
                gate_copy(6)
                unit_hi()
                gate_copy(7)
                level_exp(5)
                act.wait_ge(chunk_ready, CHUNK_NO["gate", 8 * l + 7] + 1)
                unit_hi()
                act.wait_ge(kdec_ready, l + 1)
                f(e_t[:, :, :], b_t[:, :, :], ACT.Exp).then_inc(e_exp, 1)
                if l:
                    act.wait_ge(kv_stored, 16 * 2 * l)
                kv_copy(0, 5)
                for t, (t0, rows) in enumerate(TILES):
                    b = take("kdt")
                    f(kd_tok[0:rows, t, :], ps[0:rows, b, :], ACT.Copy).then_inc(act_emptied, 1)
                kv_copy(5, 5)
                act.wait_ge(lvl_taken, 6 * (l + 1))
                act.wait_ge(work_zeroed, l + 1)
                for blk in range(4):
                    r0 = CH * blk
                    nt = 3 if blk == 0 else 2
                    for pr in range(2):
                        for t in range(nt):
                            ins = f(a_full[r0:r0 + CH, t, :, pr, r0:r0 + CH], a_comp[r0:r0 + CH, pr, t, :, :], ACT.Copy)
                ins.then_inc(a_ready, 1)
                f(gate[0:DV, :, :], gate[0:DV, :, :], ACT.Silu).then_inc(gate_silu, 1)
                kv_copy(10, 6)
                for h in range(HEADS):
                    act.wait_ge(o_ready, 8 * l + h + 1)
                    if h == 0:
                        act.wait_ge(a_ready, l + 1)
                        act.wait_ge(qdec_ready, l + 1)
                    f(osq[0:DV, h, :], ps[0:DV, 4 + h % 4, 0:T], ACT.Square).then_inc(osq_ready, 1)
                    f(o_t[0:DV, h, :], ps[0:DV, 4 + h % 4, 0:T], ACT.Copy).then_inc(o_taken, 1)
                for h in range(HEADS):
                    b = take("oss")
                    f(osq[0:DV, h, :], ps[0:DV, b, 0:T], ACT.Ln, scale=1.0 / DV, bias=epsc[0:DV, 0:1]).then_inc(act_emptied, 1)
                act.wait_ge(act_emptied, emptied("oss", 8 * l + 7))
                for h in range(HEADS):
                    f(osq[0:DV, h, :], osq[0:DV, h, :], ACT.Exp, scale=-0.5).then_inc(ors_ready, 1)
                norm(3 * l + 1, added("out", 8 * l), {6: 1, 8: 1})
                for j in range(8):
                    b = take("wq")
                    f(qx[:, j, :], ps[:, b, 0:T], ACT.Copy).then_inc(act_emptied, 1)
                    if j % 2:
                        unit_hi()

                def exps(t):
                    rows = TILES[t][1]
                    act.wait_ge(mx_ready, 3 * l + t + 1)
                    if t == 2:
                        act.wait_ge(chunk_ready, CHUNK_NO["pt", 6 * l + 1] + 1)
                    for h in range(4):
                        bank = (6 if t == 1 else 4) + h // 2
                        ins_ = f(prob[0:rows, t % 2, h, :], ps[0:rows, bank, MEM * (h % 2):MEM * (h % 2) + MEM], ACT.Exp,
                                 scale=1.0 / 16, bias=att[0:rows, t % 2, 4 + h:5 + h],
                                 accum_out=att[0:rows, t % 2, 8 + h:9 + h])
                    ins_.then_inc(ex_ready, 1)

                def turn_copy(t):
                    t0, rows = TILES[t]
                    for g in range(2):
                        b_ = take("pt")
                        f(pt[:, 4 * g:4 * g + 4, t0:t0 + rows],
                          ps[:, b_, :].rearrange("p (j m) -> p j m", m=P)[:, :, 0:rows], ACT.Copy).then_inc(act_emptied, 1)

                exps(0)
                exps(1)
                turn_copy(0)
                exps(2)
                turn_copy(1)
                turn_copy(2)
                for d in range(KD):
                    c = CHUNK_NO["ox", 8 * l + d]
                    act.wait_ge(chunk_ready, c + 1)
                    f(h_hi[:, d, :], ps[:, c % 4, 0:T], ACT.Copy).then_inc(h_hi_done, 1)
                norm(3 * l + 2, added("wo", 8 * l), {2: 1, 4: 1, 6: 1, 8: 1} if l == 0 else {2: 1, 4: 1})
                if l == 0:
                    for step in range(STEPS):
                        for i in (2 * step, 2 * step + 1):
                            b = take("h1")
                            if step:
                                act.wait_ge(dve_emptied, emptied("h3", i - 2))
                            f(sil0[:, i % 2, :], ps[:, b, 0:T], ACT.Silu).then_inc(act_emptied, 1)
                        unit_hi(2)
                        for i in (2 * step, 2 * step + 1):
                            act.wait_ge(dve_emptied, emptied("h3", i))
                            f(ff_hi[:, i, :], prod[:, i % 2, :], ACT.Copy).then_inc(ff_hi_done, 1)

            act.wait_ge(htok_zero, 1)
            for t, (t0, rows) in enumerate(TILES):
                for g in range(2):
                    b = take("htok")
                    f(htok[0:rows, t, 512 * g:512 * g + 512], ps[0:rows, b, :], ACT.Copy).then_inc(act_emptied, 1)
            act.wait_ge(gap_ready, 1)
            f(cols[:, 6:9], cols[:, 6:9], ACT.Exp).then_inc(gexp_ready, 1)
            act.wait_ge(kv_stored, 16 * 2 * LAYERS)

            def gather_hi(n):
                act.wait_ge(gathered, n)
                f(hg_hi[:, 0:5, :], ps[:, 5, 0:5 * C].rearrange("p (j m) -> p j m", m=C), ACT.Copy)
                f(hg_hi[:, 5:8, :], ps[:, 7, 0:3 * C].rearrange("p (j m) -> p j m", m=C), ACT.Copy).then_inc(hg_hi_done, 1)


            def weight_hi(it, u):
                act.wait_ge(moe_in[moe_slot(u)], it * (16 * UNITS_E // RING) + 16 * (u // RING + 1))
                act.wait_ge(w_used, it * UNITS_E + u + 1)
                f(view(w_hi, (u % SPLITS) * SLOT, SLOT), view(ring, moe_slot(u) * SLOT, SLOT),
                  ACT.Copy).then_inc(hi_done, 1)

            def expert(it, last_one):
                def silu(s):
                    act.wait_ge(w_used, it * UNITS_E + unit_of(1, s) + 1 + SPLITS)
                    f(sil[0:C, s % 2, :], ps[0:C, s % 2, 0:256], ACT.Silu).then_inc(silu_ready, 1)

                def act_hi(s):
                    act.wait_ge(a_turned, it * STEPS + s + 1)
                    f(a_hi[:, s % 2, :, :], ps[:, 4, 0:2 * C].rearrange("p (j m) -> p j m", m=C),
                      ACT.Copy).then_inc(a_hi_done, 1)

                weight_hi(it, 3)
                silu(0)
                weight_hi(it, 4)
                weight_hi(it, 5)
                silu(1)
                act.wait_ge(sel_used, it + 1)
                f(selT[0:C, :], ps[0:C, 6, 0:T], ACT.Copy).then_inc(selT_ready, 1)
                weight_hi(it, 6)
                act_hi(0)
                for s in range(2, STEPS - 1):
                    weight_hi(it, 3 * s + 1)
                    silu(s)
                    weight_hi(it, 3 * s + 2)
                    act_hi(s - 1)
                    weight_hi(it, 3 * s + 3)
                weight_hi(it, UNITS_E - 2)
                silu(STEPS - 1)
                weight_hi(it, UNITS_E - 1)
                act_hi(STEPS - 2)
                act_hi(STEPS - 1)
                if not last_one:
                    gather_hi(it + 2)
                    for u in range(SPLITS):
                        weight_hi(it + 1, u)

            for u in range(SPLITS):
                weight_hi(0, u)
            act.wait_ge(rounds_ready, 1)
            more = act.value_load(more_rounds[0:1, 0:1], min_val=0, max_val=MAXR - 1)
            gather_hi(1)
            with act.Fori(0, more * NE + (NE - 1)) as it:
                expert(it, False)
            expert(more * NE + (NE - 1), True)
            norm(3 * LAYERS, lambda d: act.wait_ge(scat_added, more * (NE * KD) + NE * KD + d + 1))

        @block.vector
        def _(dve):
            st = {"c": 0, "s": 0, "m": 0}
            V = nc.vector

            def link(ins):
                st["s"] += 1
                ins.then_inc(dve_step, 1)
                dve.wait_ge(dve_step, st["s"])

            def take(tag):
                while PLAN[st["c"]][1] != "V":
                    st["c"] += 1
                assert PLAN[st["c"]][0] == tag, (PLAN[st["c"]], tag)
                c = st["c"]
                dve.wait_ge(chunk_ready, c + 1)
                st["c"] += 1
                return c % 4

            def unit_lo(count=1):
                for _ in range(count):
                    m = st["m"]
                    n = SPLIT_UNITS[m]
                    st["m"] += 1
                    dve.wait_ge(dw_hi_done, m + 1)
                    V.tensor_tensor(view(dw_lo, (n % DSLOTS) * SLOT, unit_words(n)), slot(n, unit_words(n)),
                                    view(hi_place(n, m), 0, unit_words(n)).bitcast(F32), ALU.subtract).then_inc(dw_split, 1)

            def add_residual(tag, before={}):
                for d in range(KD):
                    unit_lo(before.get(d, 0))
                    b_ = take(tag)
                    V.tensor_tensor(xT[:, d, :], xT[:, d, :], ps[:, b_, 0:T], ALU.add).then_inc(dve_emptied, 1)
                unit_lo(before.get(KD, 0))

            def norm(i, gains):
                def low_part(k):
                    dve.wait_ge(h_hi_done, H_BASE[i] + k + 1)
                    V.tensor_tensor(h_lo[:, k, :], hT[:, k, :], h_hi[:, k, :].bitcast(F32), ALU.subtract
                                    ).then_inc(h_split, 1)

                dve.wait_ge(rstd_ready, i + 1)
                for k in range(KD):
                    V.scalar_tensor_tensor(out=hT[:, k, :], in0=xT[:, k, :], scalar=par[:, gains + k:gains + k + 1],
                                           in1=rstd[:, :], op0=ALU.mult, op1=ALU.mult).then_inc(normed, 1)
                    if i in SPLIT_NORM and k:
                        low_part(k - 1)
                if i in SPLIT_NORM:
                    low_part(KD - 1)

            V.memset(stage2[:, :], 0.0).then_inc(zeroed, 1)
            V.memset(epsc[:, :], EPS).then_inc(drv_ready, 1)
            V.memset(wqk[:, :, :, :], 0.0).then_inc(zeroed, 1)
            for t, (t0, rows) in enumerate(TILES):
                for g in range(2):
                    b = take("x")
                    V.tensor_copy(xT[:, 4 * g:4 * g + 4, t0:t0 + rows],
                                  ps[:, b, :].rearrange("p (j m) -> p j m", m=P)[:, :, 0:rows]).then_inc(dve_emptied, 1)
            dve.wait_ge(dve_emptied, emptied("x", 5))
            V.sem_inc(resid_done, 1)
            b = take("par")
            link(V.tensor_copy(par[:, :], ps[:, b, 0:124]))
            V.sem_inc(dve_emptied, 1)
            b = take("par")
            link(V.tensor_copy(par2[:, :], ps[:, b, 0:20]))
            V.sem_inc(dve_emptied, 1)
            for l in range(LAYERS):
                norm(3 * l, c_mix + 8 * l)
                if l == 0:
                    lb = par[:, c_lb:c_lb + 4]
                    lam = par[:, c_lam:c_lam + 4]
                    link(V.tensor_tensor(drv[:, 40:42], lb[:, 0:2], lb[:, 2:4], ALU.max))
                    link(V.tensor_tensor(drv[:, 32:34], lb[:, 0:2], drv[:, 40:42], ALU.subtract))
                    link(V.tensor_tensor(drv[:, 34:36], lb[:, 2:4], drv[:, 40:42], ALU.subtract))
                    link(V.tensor_scalar(drv[:, 40:44], lam, -1.0, None, ALU.mult))
                    link(V.tensor_tensor(drv[:, 36:40], lam, drv[:, 40:44], ALU.max))
                    link(V.tensor_scalar(drv[:, 44:48], drv[:, 40:44], 0.0, None, ALU.max))
                    V.sem_inc(drv_ready, 1)
                    dve.wait_ge(const_ok, 2)
                    s_i, t_i = view(low, 0, CH).bitcast(I32), view(low, 64, CH).bitcast(I32)
                    x_i, g_f = view(low, 128, CH).bitcast(I32), view(low, 192, CH)
                    m_f = view(low, 256, CH)
                    link(V.tensor_scalar(s_i, s_i, CH - 1, None, ALU.bitwise_and))
                    link(V.tensor_tensor(x_i, s_i, t_i, ALU.bitwise_xor))
                    link(V.tensor_tensor(g_f, t_i, s_i, ALU.is_gt))
                    link(V.tensor_scalar(masks[:, 0, :], x_i, 0.0, None, ALU.is_equal))
                    for i, h in enumerate(LEVELS):
                        link(V.scalar_tensor_tensor(out=m_f, in0=x_i, scalar=float(h), in1=g_f, op0=ALU.is_ge, op1=ALU.mult))
                        link(V.scalar_tensor_tensor(out=masks[:, 1 + i, :], in0=x_i, scalar=float(2 * h), in1=m_f,
                                                    op0=ALU.is_lt, op1=ALU.mult))
                    dve.wait_ge(lb_exp, 1)
                    dve.wait_ge(sp_exp, 1)
                    link(V.tensor_tensor(drv[:, 40:42], drv[:, 32:34], drv[:, 34:36], ALU.add))
                    link(V.reciprocal(drv[:, 40:42], drv[:, 40:42]))
                    link(V.tensor_tensor(drv[:, 34:36], drv[:, 34:36], drv[:, 40:42], ALU.mult))
                    link(V.memset(drv[:, 32:34], 0.0))
                    link(V.tensor_scalar(drv[:, v_kA:v_kA + 4], drv[:, 32:36], 0.5, -0.5, ALU.mult, ALU.add))
                    link(V.tensor_scalar(drv[:, v_kB:v_kB + 4], drv[:, 32:36], -0.5, 0.5, ALU.mult, ALU.add))
                    link(V.tensor_scalar(drv[:, v_fb:v_fb + 4], drv[:, 32:36], 0.5, 0.5, ALU.mult, ALU.add))
                    e_c, s_c, s2_c, p_c = drv[:, 36:40], drv[:, 48:52], drv[:, 52:56], drv[:, 56:60]
                    link(V.tensor_scalar(s_c, e_c, 2.0, None, ALU.add))
                    link(V.reciprocal(s_c, s_c))
                    link(V.tensor_tensor(s_c, s_c, e_c, ALU.mult))
                    link(V.tensor_tensor(s2_c, s_c, s_c, ALU.mult))
                    link(V.tensor_scalar(p_c, s2_c, 1.0 / 17, 1.0 / 15, ALU.mult, ALU.add))
                    for n in (13, 11, 9, 7, 5, 3, 1):
                        link(V.tensor_tensor(p_c, p_c, s2_c, ALU.mult))
                        link(V.tensor_scalar(p_c, p_c, 1.0 / n, None, ALU.add))
                    link(V.tensor_tensor(p_c, p_c, s_c, ALU.mult))
                    link(V.tensor_scalar(p_c, p_c, 2.0, None, ALU.mult))
                    link(V.tensor_tensor(p_c, p_c, drv[:, 44:48], ALU.add))
                    link(V.tensor_scalar(drv[:, v_sp:v_sp + 4], p_c, -4.0, None, ALU.mult))
                    link(V.tensor_scalar(drv[:, v_br:v_br + 8], par[:, c_br:c_br + 8], 0.5, None, ALU.mult))
                V.memset(xc[:, :, 0:3], 0.0)
                link(V.tensor_copy(xc[:, :, 3 + TP:6 + TP],
                                   par[:, c_c0 + 6 * l:c_c0 + 6 * l + 6].rearrange("p (j k) -> p k j", k=2)))
                dve.wait_ge(act_emptied, emptied("rx", 2 * l + 1))
                for j in range(2):
                    cw = c_cw + 8 * l + j
                    for x0, u0, n in ((0, 0, TP), (3 + TP, TP, TS)):
                        V.tensor_scalar(u_t[:, j, u0:u0 + n], xc[:, j, x0:x0 + n], par[:, cw:cw + 1],
                                        par[:, c_cb + 2 * l + j:c_cb + 2 * l + j + 1], ALU.mult, ALU.add
                                        ).then_inc(dve_step, 1)
                        st["s"] += 1
                for i in range(1, CONV):
                    dve.wait_ge(dve_step, st["s"])
                    for j in range(2):
                        cw = c_cw + 8 * l + 2 * i + j
                        for x0, u0, n in ((0, 0, TP), (3 + TP, TP, TS)):
                            V.scalar_tensor_tensor(out=u_t[:, j, u0:u0 + n], in0=xc[:, j, x0 + i:x0 + i + n],
                                                   scalar=par[:, cw:cw + 1], in1=u_t[:, j, u0:u0 + n],
                                                   op0=ALU.mult, op1=ALU.add).then_inc(dve_step, 1)
                            st["s"] += 1
                dve.wait_ge(dve_step, st["s"])
                V.sem_inc(u_ready, 1)
                for g, x0 in enumerate((TP, 3 + TP + TS)):
                    V.tensor_copy(small[:, 8 + 12 * g + 6 * l:14 + 12 * g + 6 * l].rearrange("p (j k) -> p k j", k=2),
                                  xc[:, :, x0:x0 + 3])
                dve.wait_ge(act_emptied, emptied("hf", 2 * l + 1))
                for j in range(2):
                    c_ = 2 * l + j
                    V.tensor_scalar(k_t[:, 2 + j, :], e_t[:, 2 + j, :], drv[:, v_kA + c_:v_kA + c_ + 1],
                                    drv[:, v_kB + c_:v_kB + c_ + 1], ALU.mult, ALU.add)
                    link(V.tensor_scalar(ql_t[:, 2 + j, :], e_t[:, 2 + j, :], drv[:, v_kB + c_:v_kB + c_ + 1],
                                         drv[:, v_fb + c_:v_fb + c_ + 1], ALU.mult, ALU.add))
                V.tensor_scalar(ql_t[:, 2:4, :], ql_t[:, 2:4, :], 1e-19, None, ALU.max).then_inc(hgf_ready, 1)
                if l == 0:
                    dve.wait_ge(act_emptied, emptied("mem", 3))
                for k in range(KD):
                    ins = V.tensor_scalar(memg[:, k, :], memT[:, k, :], par[:, c_mem + 8 * l + k:c_mem + 8 * l + k + 1],
                                          None, ALU.mult)
                ins.then_inc(memg_ready, 1)
                dve.wait_ge(ri_used, l + 1)
                for j in range(2):
                    c_ = v_sp + 2 * l + j
                    ins = V.tensor_scalar(la[:, j, :], la[:, j, :], drv[:, c_:c_ + 1], drv[:, c_:c_ + 1], ALU.mult, ALU.add)
                ins.then_inc(la_ready, 1)
                link(V.tensor_scalar(it_[:, :, :], it_[:, :, :], 0.5, 0.5, ALU.mult, ALU.add))
                link(V.tensor_tensor(it_[:, :, :], it_[:, :, :], u_t[:, :, :], ALU.mult))
                dve.wait_ge(gla_ln, l + 1)
                for j in range(2):
                    c_ = 16 + 2 * l + j
                    ins = V.tensor_scalar(kl_t[:, j, :], ps[:, 4 + j, 0:T], par2[:, c_:c_ + 1], 0.0, ALU.add, ALU.min)
                link(ins)
                link(V.tensor_tensor(kl_t[:, 0:2, :], kl_t[:, 0:2, :], e_t[:, 0:2, :], ALU.subtract))
                link(V.tensor_scalar(kl_t[:, 0:2, :], kl_t[:, 0:2, :], 1.0 / 16, None, ALU.mult))
                dve.wait_ge(hg_ln, l + 1)
                for pr in range(PAIRS):
                    ins = V.tensor_tensor_scan(out=b_t[:, pr, :], data0=restart[:, :], data1=kl_t[:, pr, :], initial=0.0,
                                               op0=ALU.mult, op1=ALU.add)
                link(ins)
                link(V.memset(ql_t[:, 0:2, :], 0.0))

                def blocks(x, s):
                    return x.rearrange("p a (n s) -> p (a n) s", s=s)

                def level_e(i):
                    h = LEVELS[i]
                    bv, ev = blocks(b_t, 2 * h), blocks(e_t, 2 * h)
                    n = PAIRS * T // (2 * h)
                    mid = bv[:, :, h - 1:h].to_broadcast([P, n, h])
                    V.tensor_tensor(ev[:, :, 0:h], mid, bv[:, :, 0:h], ALU.subtract)
                    V.tensor_tensor(ev[:, :, h:2 * h], bv[:, :, h:2 * h], mid, ALU.subtract).then_inc(e_ready, 1)

                def level_qk(i):
                    h = LEVELS[i]
                    dve.wait_ge(e_exp, 7 * l + i + 1)
                    if i:
                        dve.wait_ge(lvl_ready, 6 * l + i + 1)
                    ev = blocks(e_t, 2 * h)
                    V.tensor_tensor(blocks(kl_t, 2 * h)[:, :, 0:h], blocks(k_t, 2 * h)[:, :, 0:h], ev[:, :, 0:h], ALU.mult)
                    ins_ = V.tensor_tensor(blocks(ql_t, 2 * h)[:, :, h:2 * h], blocks(q_t, 2 * h)[:, :, h:2 * h],
                                           ev[:, :, h:2 * h], ALU.mult)
                    ins_.then_inc(lvl_qk, 1)
                    dve.wait_ge(lvl_qk, 5 * l + i + 1)

                def level_take(idx):
                    dve.wait_ge(lvl_ready, 6 * l + idx + 1)
                    b0 = 4 if idx % 2 else 6
                    for pr in range(2):
                        V.copy_predicated(a_comp[:, pr, 0:2, :, :].rearrange("p t g c -> p (t g) c"),
                                          masks[:, idx:idx + 1, :].to_broadcast([P, 8, CH]),
                                          ps[:, b0 + pr, 0:8 * CH].rearrange("p (g c) -> p g c", c=CH))
                        ins_ = V.copy_predicated(a_comp[0:CH, pr, 2, :, :],
                                                 masks[0:CH, idx:idx + 1, :].to_broadcast([CH, 4, CH]),
                                                 ps[0:CH, b0 + pr, 8 * CH:12 * CH].rearrange("p (g c) -> p g c", c=CH))
                    ins_.then_inc(lvl_taken, 1)
                    dve.wait_ge(lvl_taken, 6 * l + idx + 1)

                level_e(0)
                link(V.memset(a_comp[:, :, :, :, :], 0.0))
                dve.wait_ge(beta_ready, 2 * l + 1)
                link(V.tensor_tensor(u_t[:, :, :], la[:, :, :], la[:, :, :], ALU.mult))
                link(V.scalar_tensor_tensor(out=tn[:, :, :], in0=u_t[:, :, :], scalar=1.0, in1=tn[:, :, :],
                                            op0=ALU.add, op1=ALU.mult))
                V.tensor_scalar(tn[:, :, :], tn[:, :, :], 1e-12, None, ALU.max).then_inc(beta2_ready, 1)
                level_take(0)
                level_qk(0)
                level_e(1)
                dve.wait_ge(beta_ready, 2 * l + 2)
                link(V.tensor_tensor(it_[:, :, :], it_[:, :, :], tn[:, :, :], ALU.mult))
                for j in range(2):
                    V.tensor_tensor_scan(out=tn[:, j, 0:TP], data0=la[:, j, 0:TP], data1=it_[:, j, 0:TP], initial=0.0,
                                         op0=ALU.mult, op1=ALU.add)
                    h0 = c_h0 + 2 * l + j
                    ins = V.tensor_tensor_scan(out=tn[:, j, TP:T], data0=la[:, j, TP:T], data1=it_[:, j, TP:T],
                                               initial=par[:, h0:h0 + 1], op0=ALU.mult, op1=ALU.add)
                link(ins)
                for g, t_ in enumerate((TP - 1, T - 1)):
                    V.tensor_copy(small[:, 4 * g + 2 * l:4 * g + 2 * l + 2], tn[:, :, t_])
                link(V.tensor_tensor(la[:, :, :], tn[:, :, :], gb[:, :, :], ALU.mult))
                level_take(1)
                for i in range(1, 5):
                    level_qk(i)
                    if i < 4:
                        level_e(i + 1)
                    else:
                        bv, ev = blocks(b_t, CH), blocks(e_t, CH)
                        V.tensor_tensor(ev[:, :, :], bv[:, :, CH - 1:CH].to_broadcast([P, PAIRS * NCH, CH]), bv[:, :, :],
                                        ALU.subtract).then_inc(e_ready, 1)
                        unit_lo(2)
                    if i == 3:
                        dve.wait_ge(mg_hi_done, l + 1)
                        V.tensor_tensor(mg_lo[:, :, :], memg[:, :, :], mg_hi[:, :, :].bitcast(F32),
                                        ALU.subtract).then_inc(mg_split, 1)
                    level_take(i + 1)
                dve.wait_ge(e_exp, 7 * l + 6)
                V.tensor_tensor(kl_t[:, :, :], k_t[:, :, :], e_t[:, :, :], ALU.mult).then_inc(kdec_ready, 1)
                dve.wait_ge(e_exp, 7 * l + 7)
                V.tensor_tensor(ql_t[:, :, :], q_t[:, :, :], e_t[:, :, :], ALU.mult).then_inc(qdec_ready, 1)
                unit_lo(2)
                dve.wait_ge(work_zeroed, l + 1)
                dve.wait_ge(layer_in, 16 * (9 + 16 * (l + 1)))
                if l:
                    dve.wait_ge(stored, 16 * 16 * l)
                eb = e_t.rearrange("p a (c t) -> p a c t", t=CH)
                for c in range(NCH):
                    s_in = s_all[:, c, :, :] if c < 8 else s_init[:, :, :]
                    s_out = s_all[:, c + 1, :, :] if c < 7 else s_fin[:, c - 7, :, :]
                    link(V.tensor_tensor(s_out, s_in, eb[:, :, c, CH - 1:CH].to_broadcast([P, PAIRS, DV]), ALU.mult))
                    dve.wait_ge(kv_ready, 9 * l + c + 1)
                    V.tensor_tensor(s_out, s_out, ps[:, 4 + c % 4, 0:PAIRS * DV].rearrange("p (a v) -> p a v", v=DV),
                                    ALU.add).then_inc(kv_taken, 1)
                    dve.wait_ge(kv_taken, 9 * l + c + 1)
                    if c in (4, 6):
                        unit_lo()
                unit_lo(2)
                dve.wait_ge(gate_silu, l + 1)
                done = st["s"]
                for h in range(HEADS):
                    col = 4 * l + h if h < 4 else 8 + 4 * l + h - 4
                    dve.wait_ge(o_taken, 8 * l + h + 1)
                    V.scalar_tensor_tensor(out=o_t[0:DV, h, :], in0=o_t[0:DV, h, :], scalar=par2[0:DV, col:col + 1],
                                           in1=gate[0:DV, h, :], op0=ALU.mult, op1=ALU.mult).then_inc(dve_step, 1)
                    st["s"] += 1
                for h in range(HEADS):
                    dve.wait_ge(dve_step, done + h + 1)
                    dve.wait_ge(ors_ready, 8 * l + h + 1)
                    V.tensor_tensor(o_t[0:DV, h, :], o_t[0:DV, h, :], osq[0:DV, h, :], ALU.mult).then_inc(mix_ready, 1)
                add_residual("out", {6: 1, 8: 1})
                norm(3 * l + 1, c_xa + 8 * l)
                unit_lo(3)
                for g in range(2):
                    for t in range(2):
                        for q4 in range(2):
                            b = take("kt")
                            V.tensor_copy((kts if g else ktp)[:, 4 * q4:4 * q4 + 4, P * t:P * t + P],
                                          ps[:, b, :].rearrange("p (j m) -> p j m", m=P)).then_inc(dve_emptied, 1)

                def maxima(t):
                    rows = TILES[t][1]
                    dve.wait_ge(sc_ready, 3 * l + t + 1)
                    b0 = 6 if t == 1 else 4
                    link(V.tensor_reduce(att[0:rows, t % 2, 0:4],
                                         ps[0:rows, b0:b0 + 2, :].rearrange("p b (h m) -> p (b h) m", m=MEM),
                                         AX.X, ALU.max))
                    V.tensor_scalar(att[0:rows, t % 2, 4:8], att[0:rows, t % 2, 0:4], -1.0 / 16, None,
                                    ALU.mult).then_inc(mx_ready, 1)

                def divide(t):
                    rows = TILES[t][1]
                    dve.wait_ge(ex_ready, 3 * l + t + 1)
                    link(V.reciprocal(att[0:rows, t % 2, 12:16], att[0:rows, t % 2, 8:12]))
                    for h in range(4):
                        ins_ = V.tensor_scalar(prob[0:rows, t % 2, h, :], prob[0:rows, t % 2, h, :],
                                               att[0:rows, t % 2, 12 + h:13 + h], None, ALU.mult)
                    ins_.then_inc(pr_ready, 1)
                    dve.wait_ge(pr_ready, 3 * l + t + 1)

                unit_lo()
                maxima(0)
                maxima(1)
                divide(0)
                maxima(2)
                divide(1)
                divide(2)
                for d in range(KD):
                    b = take("ox")
                    dve.wait_ge(h_hi_done, KD * (3 * l + 1) + d + 1)
                    V.tensor_tensor(h_lo[:, d, :], ps[:, b, 0:T], h_hi[:, d, :].bitcast(F32), ALU.subtract
                                    ).then_inc(dve_emptied, 1)
                add_residual("wo", {2: 1, 4: 1, 6: 1, 8: 1} if l == 0 else {2: 1, 4: 1})
                norm(3 * l + 2, c_ff + 8 * l)
                if l == 0:
                    for step in range(STEPS):
                        unit_lo()
                        for i in (2 * step, 2 * step + 1):
                            b = take("h3")
                            dve.wait_ge(act_emptied, emptied("h1", i))
                            if step:
                                dve.wait_ge(ff_split, i - 1)
                            V.tensor_tensor(prod[:, i % 2, :], sil0[:, i % 2, :], ps[:, b, 0:T],
                                            ALU.mult).then_inc(dve_emptied, 1)
                        unit_lo()
                        for i in (2 * step, 2 * step + 1):
                            dve.wait_ge(ff_hi_done, i + 1)
                            V.tensor_tensor(ff_lo[:, i, :], prod[:, i % 2, :], ff_hi[:, i, :].bitcast(F32),
                                            ALU.subtract).then_inc(ff_split, 1)
                    add_residual("dn", {d: 2 for d in range(KD - 1)})

            V.memset(htok[:, 2, :], 0.0).then_inc(htok_zero, 1)
            link(V.memset(lgt[:, :, :], 0.0))
            b = take("lg")
            V.tensor_copy(lgt[:, 0:2, :], ps[:, b, 0:2 * NE].rearrange("p (t e) -> p t e", e=NE))
            link(V.tensor_copy(lgt[0:TS, 2, :], ps[0:TS, b, 2 * NE:3 * NE]))
            V.sem_inc(dve_emptied, 1)
            for i, oh in enumerate((oh1, oh2)):
                link(V.tensor_reduce(cols[:, 3 * i:3 * i + 3], lgt[:, :, :], AX.X, ALU.max))
                top = cols[:, 3 * i:3 * i + 3].rearrange("p (t e) -> p t e", e=1).to_broadcast([P, 3, NE])
                link(V.tensor_tensor(tmp8[:, :, :], lgt[:, :, :], top, ALU.is_equal))
                link(V.tensor_tensor(tmp8[:, :, :], tmp8[:, :, :], iota_e[:, :, :], ALU.mult))
                link(V.tensor_reduce(cols[:, 12:15], tmp8[:, :, :], AX.X, ALU.min))
                first = cols[:, 12:15].rearrange("p (t e) -> p t e", e=1).to_broadcast([P, 3, NE])
                link(V.tensor_tensor(oh, iota_e[:, :, :], first, ALU.is_equal))
                if i == 0:
                    link(V.scalar_tensor_tensor(out=lgt[:, :, :], in0=oh, scalar=-3e38, in1=lgt[:, :, :],
                                                op0=ALU.mult, op1=ALU.add))
            link(V.tensor_tensor(cols[:, 6:9], cols[:, 3:6], cols[:, 0:3], ALU.subtract))
            V.sem_inc(gap_ready, 1)
            link(V.tensor_tensor(msel[:, :, :], oh1, oh2, ALU.add))
            link(V.memset(msel[TS:64, 2, :], 0.0))
            link(V.memset(msel[64:P, 2, :], 0.0))
            V.sem_inc(msel_ready, 1)
            dve.wait_ge(gexp_ready, 1)
            link(V.tensor_scalar(cols[:, 9:12], cols[:, 6:9], 1.0, None, ALU.add))
            link(V.reciprocal(cols[:, 9:12], cols[:, 9:12]))
            link(V.tensor_tensor(cols[:, 6:9], cols[:, 6:9], cols[:, 9:12], ALU.mult))
            g1 = cols[:, 9:12].rearrange("p (t e) -> p t e", e=1).to_broadcast([P, 3, NE])
            g2 = cols[:, 6:9].rearrange("p (t e) -> p t e", e=1).to_broadcast([P, 3, NE])
            link(V.tensor_tensor(gd[:, :, :], oh1, g1, ALU.mult))
            link(V.tensor_tensor(tmp8[:, :, :], oh2, g2, ALU.mult))
            link(V.tensor_tensor(gd[:, :, :], gd[:, :, :], tmp8[:, :, :], ALU.add))
            b = take("rank")
            link(V.scalar_tensor_tensor(out=tmp8[:, :, :], in0=ps[:, b, 0:3 * NE].rearrange("p (t e) -> p t e", e=NE),
                                        scalar=1024.0, in1=msel[:, :, :], op0=ALU.add, op1=ALU.mult))
            for r in range(MAXR + 1):
                link(V.tensor_scalar(posr[:, :, NE * r:NE * r + NE], tmp8[:, :, :], -1024.0 - C * r, None, ALU.add))
            link(V.tensor_reduce(cols[0:1, 16:17], ps[0:1, b, 3 * NE:4 * NE], AX.X, ALU.max))
            V.sem_inc(dve_emptied, 1)
            link(V.tensor_scalar(cols[0:1, 17:18], cols[0:1, 16:17], float(C), None, ALU.is_gt))
            for r in range(2, MAXR):
                link(V.tensor_scalar(cols[0:1, 18:19], cols[0:1, 16:17], float(C * r), None, ALU.is_gt))
                link(V.tensor_tensor(cols[0:1, 17:18], cols[0:1, 17:18], cols[0:1, 18:19], ALU.add))
            link(V.tensor_copy(more_rounds[0:1, 0:1], cols[0:1, 17:18]))
            V.sem_inc(rounds_ready, 1)
            more = dve.value_load(more_rounds[0:1, 0:1], min_val=0, max_val=MAXR - 1)
            dve.wait_ge(act_emptied, emptied("htok", 5))
            V.memset(ps[0:C, 2:4, :], 0.0)
            V.memset(gs[0:C, :], 0.0)
            link(V.memset(selT[0:C, :], 0.0))

            def gather_lo(n):
                dve.wait_ge(hg_hi_done, n)
                V.tensor_tensor(hg_lo[:, 0:5, :], ps[:, 5, 0:5 * C].rearrange("p (j m) -> p j m", m=C),
                                hg_hi[:, 0:5, :].bitcast(F32), ALU.subtract)
                V.tensor_tensor(hg_lo[:, 5:8, :], ps[:, 7, 0:3 * C].rearrange("p (j m) -> p j m", m=C),
                                hg_hi[:, 5:8, :].bitcast(F32), ALU.subtract).then_inc(hg_ready, 1)

            def scale_y(n):
                dve.wait_ge(w_used, n * UNITS_E + SPLITS)
                V.tensor_scalar(y_sb[0:C, :], ps[0:C, 2:4, :].rearrange("p b n -> p (b n)"), gs[0:C, 0:1], None,
                                ALU.mult).then_inc(y_scaled, 1)

            def add_y(n):
                for d in range(KD):
                    dve.wait_ge(scat_ready, n * KD + d + 1)
                    V.tensor_tensor(xT[:, d, :], xT[:, d, :], ps[:, 4 + d % 4, 0:T], ALU.add).then_inc(scat_added, 1)

            dve.wait_ge(const_ok, 3)
            V.tensor_copy(gcol[:, :].rearrange("p (t e) -> p t e", e=1), gd[:, :, 0:1])
            for t in range(3):
                ins = V.tensor_scalar(sel[:, t, :], iota_c[:, :], posr[:, t, 0:1], None, ALU.is_equal)
            ins.then_inc(sel_ready, 1)

            def weight_lo(it, u):
                dve.wait_ge(hi_done, it * UNITS_E + u + 1)
                off = (u % SPLITS) * SLOT
                V.tensor_tensor(view(w_lo, off, SLOT), view(ring, moe_slot(u) * SLOT, SLOT),
                                view(w_hi, off, SLOT).bitcast(F32), ALU.subtract).then_inc(lo_done, 1)

            def expert(it, last_one):
                def multiply(s):
                    dve.wait_ge(silu_ready, it * STEPS + s + 1)
                    V.tensor_tensor(a_tok[0:C, s % 2, :], sil[0:C, s % 2, :], ps[0:C, s % 2, 256:512],
                                    ALU.mult).then_inc(act_ready, 1)

                def act_lo(s):
                    dve.wait_ge(a_hi_done, it * STEPS + s + 1)
                    V.tensor_tensor(a_lo[:, s % 2, :, :], ps[:, 4, 0:2 * C].rearrange("p (j m) -> p j m", m=C),
                                    a_hi[:, s % 2, :, :].bitcast(F32), ALU.subtract).then_inc(a_split, 1)

                scale_y(it)
                weight_lo(it, 2)
                add_y(it)
                weight_lo(it, 3)
                multiply(0)
                weight_lo(it, 4)
                weight_lo(it, 5)
                multiply(1)
                dve.wait_ge(selT_ready, it + 1)
                V.tensor_copy(gs[0:C, :], ps[0:C, 6, 384:385])
                if not last_one:
                    e = dve.snap((it + 1) & (NE - 1), min_val=0, max_val=NE - 1)
                    V.tensor_copy(gcol[:, :].rearrange("p (t e) -> p t e", e=1), gd[:, :, bass.ds(e, 1)])
                    for t in range(3):
                        ins = V.tensor_scalar(sel[:, t, :], iota_c[:, :], posr[:, t, bass.ds(it + 1, 1)], None, ALU.is_equal)
                    ins.then_inc(sel_ready, 1)
                weight_lo(it, 6)
                act_lo(0)
                for s in range(2, STEPS - 1):
                    weight_lo(it, 3 * s + 1)
                    multiply(s)
                    weight_lo(it, 3 * s + 2)
                    act_lo(s - 1)
                    weight_lo(it, 3 * s + 3)
                weight_lo(it, UNITS_E - 2)
                multiply(STEPS - 1)
                weight_lo(it, UNITS_E - 1)
                act_lo(STEPS - 2)
                act_lo(STEPS - 1)
                if not last_one:
                    gather_lo(it + 2)
                    for u in range(SPLITS - 1):
                        weight_lo(it + 1, u)

            weight_lo(0, 0)
            weight_lo(0, 1)
            gather_lo(1)
            with dve.Fori(0, more * NE + (NE - 1)) as it:
                expert(it, False)
            expert(more * NE + (NE - 1), True)
            scale_y(more * NE + NE)
            add_y(more * NE + NE)
            norm(3 * LAYERS, c_fin)
            for t, (t0, rows) in enumerate(TILES):
                for g in range(2):
                    b = take("y")
                    V.tensor_copy(ytok[0:rows, t, 512 * g:512 * g + 512], ps[0:rows, b, :]).then_inc(dve_emptied, 1)
            b = take("small")
            V.tensor_copy(stage3[0:32, :], ps[0:32, b, 0:P]).then_inc(small_ready, 1)


_INS = ['x_prompt', 'x_sample', 'state_gla', 'state_hgrn', 'state_rglru', 'state_conv', 'cache_mem_k', 'cache_mem_v',
        'mem_prompt', 'norm_mix', 'norm_xattn', 'norm_ffn', 'norm_mem', 'norm_final', 'w_in', 'gla_wa2', 'gla_ba',
        'gla_onorm', 'hg_lb', 'hg_onorm', 'rg_conv_w', 'rg_conv_b', 'rg_wr', 'rg_br', 'rg_wi', 'rg_bi', 'rg_lambda',
        'w_out', 'xa_wq', 'xa_wk', 'xa_wv', 'xa_wo', 'ffd_w1', 'ffd_w3', 'ffd_w2', 'moe_router', 'moe_w1', 'moe_w3',
        'moe_w2']
_OUTS = [(1, 256, 1024), (1, 32, 1024), (2, 1, 4, 48, 96), (2, 1, 4, 64, 96), (2, 1, 256), (2, 1, 3, 256),
         (2, 1, 256, 4, 256), (2, 1, 256, 4, 256), (2, 1, 4, 48, 96), (2, 1, 4, 64, 96), (2, 1, 256), (2, 1, 3, 256)]


def kernel(**inputs):
    import numpy as _np
    import concourse.bacc as _bacc
    from concourse import mybir as _mybir
    from concourse.bass_utils import run_bass_kernel_spmd as _run

    nc = _bacc.Bacc("TRN2", target_bir_lowering=False, num_devices=1)
    arrays, args = {}, []
    for name in _INS:
        a = _np.ascontiguousarray(inputs[name])
        arrays[f"in_{name}_dram"] = a
        args.append(nc.dram_tensor(f"in_{name}_dram", a.shape, _mybir.dt.from_np(a.dtype), kind="ExternalInput").ap())
    for i, shape in enumerate(_OUTS):
        args.append(nc.dram_tensor(f"out_{i}_dram", shape, _mybir.dt.float32, kind="ExternalOutput").ap())
    layer_program(nc, *args)
    r = _run(nc, [arrays], core_ids=[0])
    return tuple(r.results[0][f"out_{i}_dram"] for i in range(len(_OUTS)))
```
